# Optimizing a Trainium2 kernel written in Bass

```python
import math
import jax, jax.numpy as jnp
from jax import lax
import numpy as np

D_MODEL = 1024
BATCH = 1
SEQ = 128
DEPTH = 2
DEC_BATCH = 1
DEC_SEQ = 512
PAST_LEN = 128

GRID_W = 64
CHUNK = 128
EPS = 1e-6
A_WIDTH = 256
A_GROUPS = 4
B_WIDTH = 256
CONV_W = 3
FILTER_EMB = 33
FILTER_HIDDEN = 64
FILTER_FAST_DECAY = 0.3
FILTER_SLOW_DECAY = 1.5
FILTER_TARGET = 1e-2
MLA_HEADS = 8
Q_RANK = 256
KV_RANK = 128
NOPE_DIM = 64
ROPE_DIM = 32
V_DIM = 64
ROPE_BASE = 10000.0
GATE_COLS = 3 * D_MODEL
A_COLS = 2 * A_WIDTH
B_COLS = 3 * B_WIDTH
C_COLS = Q_RANK + KV_RANK + ROPE_DIM
IN_COLS = GATE_COLS + A_COLS + B_COLS + C_COLS
PEER_HEADS = 8
N_KEYS = 128
N_EXPERTS = N_KEYS * N_KEYS
PEER_KEY_DIM = 256
PEER_TOPK = 16
PEER_BLOCK = 128

kernel_name = 'hybrid_gmlp_hyena_mla_peer_diffusion_step'

def rms_norm(x, g):
    xf = x.astype(jnp.float32)
    y = xf * lax.rsqrt(jnp.mean(xf * xf, axis=-1, keepdims=True) + EPS)
    return (y * g.astype(jnp.float32)).astype(x.dtype)

def axial_rope_tables(n_tokens, dtype):
    rows = n_tokens // GRID_W
    row = jnp.broadcast_to(jnp.arange(rows)[:, None], (rows, GRID_W)).reshape(-1)
    col = jnp.broadcast_to(jnp.arange(GRID_W)[None, :], (rows, GRID_W)).reshape(-1)
    quarter = ROPE_DIM // 4
    inv_freq = ROPE_BASE ** (-jnp.arange(quarter, dtype=jnp.float32) / quarter)
    ang = jnp.stack([row, col], axis=-1).astype(jnp.float32)[:, :, None] * inv_freq
    return jnp.cos(ang).astype(dtype), jnp.sin(ang).astype(dtype)

def apply_axial_rope(x, cos, sin):
    xr = x.reshape(x.shape[:-1] + (2, 2, ROPE_DIM // 4))
    x1, x2 = xr[..., 0, :], xr[..., 1, :]
    out = jnp.stack([x1 * cos - x2 * sin, x2 * cos + x1 * sin], axis=-2)
    return out.reshape(x.shape)

def chunk_gating_mlp(z, w_s, b_s):
    bsz, L, _ = z.shape
    z = jax.nn.gelu(z)
    u, v = jnp.split(z, 2, axis=-1)
    v = v.reshape(bsz, L // CHUNK, CHUNK, A_GROUPS, A_WIDTH // A_GROUPS)
    mixed = jnp.einsum('gpq,bnqgc->bnpgc', w_s, v) + b_s.T[:, :, None]
    return u * mixed.reshape(bsz, L, A_WIDTH)

def short_conv(z, w, b):
    L = z.shape[1]
    pad = CONV_W // 2
    zp = jnp.pad(z, ((0, 0), (pad, CONV_W - 1 - pad), (0, 0)))
    out = b
    for k in range(CONV_W):
        out = out + zp[:, k:k + L] * w[k]
    return out

def hyena_filter(L, w1, b1, w2, b2, w3):
    f32 = jnp.float32
    t = jnp.linspace(0.0, 1.0, L, dtype=f32)[:, None]
    bands = (FILTER_EMB - 1) // 2
    f = jnp.linspace(1e-4, bands - 1, bands, dtype=f32)
    w = 2.0 * math.pi * jnp.arange(L, dtype=f32)[:, None] / L
    z = jnp.concatenate([t, jnp.cos(f * w), -jnp.sin(f * w)], axis=-1)
    h = jnp.sin(z @ w1.astype(f32) + b1.astype(f32))
    h = jnp.sin(h @ w2.astype(f32) + b2.astype(f32))
    h = (h @ w3.astype(f32)).reshape(L, 2, B_WIDTH)
    deltas = jnp.abs(jnp.linspace(math.log(FILTER_TARGET) / FILTER_FAST_DECAY,
                                  math.log(FILTER_TARGET) / FILTER_SLOW_DECAY, B_WIDTH, dtype=f32))
    h = h * jnp.exp(-t * deltas)[:, None, :]
    fwd, bwd = h[:, 0], h[:, 1]
    return jnp.concatenate([fwd, jnp.zeros((1, B_WIDTH), f32), bwd[:0:-1]], axis=0)

def long_conv(u, h_circ, skip):
    L = u.shape[1]
    uf = u.astype(jnp.float32)
    U = jnp.fft.rfft(uf, n=2 * L, axis=1)
    Hf = jnp.fft.rfft(h_circ, n=2 * L, axis=0)
    y = jnp.fft.irfft(U * Hf[None], n=2 * L, axis=1)[:, :L]
    return (y + uf * skip.astype(jnp.float32)).astype(u.dtype)

def hyena_branch(z, conv_w, conv_b, w1, b1, w2, b2, w3, skip):
    z = short_conv(z, conv_w, conv_b)
    x0, x1, v = jnp.split(z, 3, axis=-1)
    h_circ = hyena_filter(z.shape[1], w1, b1, w2, b2, w3)
    return x0 * long_conv(x1 * v, h_circ, skip)

def latent_attention(q_lat, q_pe, ckv, kpe):
    bsz, Lq, H, _ = q_lat.shape
    nb = Lq // CHUNK
    scale = (NOPE_DIM + ROPE_DIM) ** -0.5

    def to_blocks(a):
        return jnp.moveaxis(a.reshape((bsz, nb, CHUNK) + a.shape[2:]), 1, 0)

    def block(args):
        ql, qp = args
        s = (jnp.einsum('bqhc,bkc->bhqk', ql, ckv) + jnp.einsum('bqhr,bkr->bhqk', qp, kpe)).astype(jnp.float32) * scale
        p = jax.nn.softmax(s, axis=-1).astype(ckv.dtype)
        return jnp.einsum('bhqk,bkc->bqhc', p, ckv)

    o = lax.map(block, (to_blocks(q_lat), to_blocks(q_pe)))
    return jnp.moveaxis(o, 0, 1).reshape(bsz, Lq, H, KV_RANK)

def peer_ffn(h, w_q, sub_keys, u_tab, v_tab):
    bsz, L, D = h.shape
    tok = h.reshape(-1, D)
    T = tok.shape[0]
    q = (tok @ w_q).reshape(T, PEER_HEADS, 2, PEER_KEY_DIM // 2)
    s = jnp.einsum('thsk,snk->thsn', q, sub_keys).astype(jnp.float32)
    sv, si = lax.top_k(s, PEER_TOPK)
    cand_s = (sv[..., 0, :, None] + sv[..., 1, None, :]).reshape(T, PEER_HEADS, PEER_TOPK * PEER_TOPK)
    cand_i = (si[..., 0, :, None] * N_KEYS + si[..., 1, None, :]).reshape(T, PEER_HEADS, PEER_TOPK * PEER_TOPK)
    top_s, top_pos = lax.top_k(cand_s, PEER_TOPK)
    idx = jnp.take_along_axis(cand_i, top_pos, axis=-1)
    g = jax.nn.softmax(top_s, axis=-1).astype(h.dtype)
    nb = T // PEER_BLOCK

    def block(args):
        tb, ib, gb = args
        a = jax.nn.gelu(jnp.einsum('tkd,td->tk', jnp.take(u_tab, ib, axis=0), tb))
        return jnp.einsum('tk,tkd->td', gb * a, jnp.take(v_tab, ib, axis=0))

    out = lax.map(block, (tok.reshape(nb, PEER_BLOCK, D),
                          idx.reshape(nb, PEER_BLOCK, PEER_HEADS * PEER_TOPK),
                          g.reshape(nb, PEER_BLOCK, PEER_HEADS * PEER_TOPK)))
    return out.reshape(bsz, L, D)

def trunk_layer(x, cond, lp, ctx_kv, rope):
    bsz, L, _ = x.shape
    mod = jax.nn.silu(cond) @ lp['w_ada'] + lp['b_ada']
    sh1, sc1, g1, sh2, sc2, g2 = jnp.split(mod[:, None, :], 6, axis=-1)
    h = rms_norm(x, lp['norm1']) * (1.0 + sc1) + sh1
    proj = h @ lp['w_in']
    c0 = GATE_COLS
    c1 = c0 + A_COLS
    c2 = c1 + B_COLS
    c3 = c2 + Q_RANK
    c4 = c3 + KV_RANK
    gates, za, zb, zq, zkv, kpe = jnp.split(proj, [c0, c1, c2, c3, c4], axis=-1)
    ya = chunk_gating_mlp(za, lp['a_ws'], lp['a_bs'])
    yb = hyena_branch(zb, lp['b_conv_w'], lp['b_conv_b'], lp['b_filt_w1'], lp['b_filt_b1'],
                      lp['b_filt_w2'], lp['b_filt_b2'], lp['b_filt_w3'], lp['b_skip'])
    q = (rms_norm(zq, lp['q_norm']) @ lp['w_uq']).reshape(bsz, L, MLA_HEADS, NOPE_DIM + ROPE_DIM)
    q_nope, q_pe = q[..., :NOPE_DIM], q[..., NOPE_DIM:]
    ckv = rms_norm(zkv, lp['kv_norm'])
    own_ckv, own_kpe = ckv, kpe
    if rope is not None:
        cos, sin = rope
        q_pe = apply_axial_rope(q_pe, cos[:, None], sin[:, None])
        kpe = apply_axial_rope(kpe, cos, sin)
    if ctx_kv is not None:
        ckv = jnp.concatenate([ckv, ctx_kv[0]], axis=1)
        kpe = jnp.concatenate([kpe, ctx_kv[1]], axis=1)
    q_lat = jnp.einsum('blhn,chn->blhc', q_nope, lp['w_uk'])
    o_lat = latent_attention(q_lat, q_pe, ckv, kpe)
    yc = jnp.einsum('blhc,chv->blhv', o_lat, lp['w_uv']).reshape(bsz, L, MLA_HEADS * V_DIM)
    ga, gb, gc = jnp.split(jax.nn.sigmoid(gates), 3, axis=-1)
    merged = ga * (ya @ lp['w_branch_a']) + gb * (yb @ lp['w_branch_b']) + gc * (yc @ lp['w_branch_c'])
    x = x + g1 * (merged @ lp['w_out'])
    h2 = rms_norm(x, lp['norm2']) * (1.0 + sc2) + sh2
    x = x + g2 * peer_ffn(h2, lp['peer_wq'], lp['peer_sub_keys'], lp['peer_u'], lp['peer_v'])
    return x, own_ckv, own_kpe

def setup_inputs(seed: int = 0) -> dict:
    key = jax.random.key(seed)
    ks = iter(jax.random.split(key, 48))
    D = D_MODEL

    def nrm(shape, scale):
        return jax.random.normal(next(ks), shape, jnp.float32) * scale

    return {
        'x_prompt': nrm((BATCH, SEQ, D), 1.0),
        'x_sample': nrm((DEC_BATCH, DEC_SEQ, D), 1.0),
        'cache_ckv': nrm((DEC_BATCH, DEPTH, PAST_LEN, KV_RANK), 1.0),
        'cache_kpe': nrm((DEC_BATCH, DEPTH, PAST_LEN, ROPE_DIM), 1.0),
        'c': nrm((DEC_BATCH, D), 1.0),
        'c_ctx': nrm((D,), 1.0),
        'w_ada': nrm((DEPTH, D, 6 * D), 0.5 * D ** -0.5),
        'b_ada': nrm((DEPTH, 6 * D), 0.02),
        'norm1': 1.0 + nrm((DEPTH, D), 0.02),
        'norm2': 1.0 + nrm((DEPTH, D), 0.02),
        'w_in': nrm((DEPTH, D, IN_COLS), D ** -0.5),
        'a_ws': nrm((DEPTH, A_GROUPS, CHUNK, CHUNK), CHUNK ** -0.5),
        'a_bs': 1.0 + nrm((DEPTH, A_GROUPS, CHUNK), 0.02),
        'b_conv_w': nrm((DEPTH, CONV_W, B_COLS), CONV_W ** -0.5),
        'b_conv_b': nrm((DEPTH, B_COLS), 0.02),
        'b_filt_w1': nrm((DEPTH, FILTER_EMB, FILTER_HIDDEN), FILTER_EMB ** -0.5),
        'b_filt_b1': nrm((DEPTH, FILTER_HIDDEN), 0.02),
        'b_filt_w2': nrm((DEPTH, FILTER_HIDDEN, FILTER_HIDDEN), FILTER_HIDDEN ** -0.5),
        'b_filt_b2': nrm((DEPTH, FILTER_HIDDEN), 0.02),
        'b_filt_w3': nrm((DEPTH, FILTER_HIDDEN, 2 * B_WIDTH), 0.05 * FILTER_HIDDEN ** -0.5),
        'b_skip': nrm((DEPTH, B_WIDTH), 0.1),
        'q_norm': 1.0 + nrm((DEPTH, Q_RANK), 0.02),
        'kv_norm': 1.0 + nrm((DEPTH, KV_RANK), 0.02),
        'w_uq': nrm((DEPTH, Q_RANK, MLA_HEADS * (NOPE_DIM + ROPE_DIM)), Q_RANK ** -0.5),
        'w_uk': nrm((DEPTH, KV_RANK, MLA_HEADS, NOPE_DIM), KV_RANK ** -0.5),
        'w_uv': nrm((DEPTH, KV_RANK, MLA_HEADS, V_DIM), KV_RANK ** -0.5),
        'w_branch_a': nrm((DEPTH, A_WIDTH, D), A_WIDTH ** -0.5),
        'w_branch_b': nrm((DEPTH, B_WIDTH, D), B_WIDTH ** -0.5),
        'w_branch_c': nrm((DEPTH, MLA_HEADS * V_DIM, D), (MLA_HEADS * V_DIM) ** -0.5),
        'w_out': nrm((DEPTH, D, D), D ** -0.5),
        'peer_wq': nrm((DEPTH, D, PEER_HEADS * PEER_KEY_DIM), D ** -0.5),
        'peer_sub_keys': nrm((DEPTH, 2, N_KEYS, PEER_KEY_DIM // 2), (PEER_KEY_DIM // 2) ** -0.5),
        'peer_u': nrm((DEPTH, N_EXPERTS, D), D ** -0.5),
        'peer_v': nrm((DEPTH, N_EXPERTS, D), PEER_HEADS ** -0.5),
        'final_norm': 1.0 + nrm((D,), 0.02),
    }

def reference(x_prompt, x_sample, cache_ckv, cache_kpe, c, c_ctx, w_ada, b_ada, norm1, norm2, w_in,
              a_ws, a_bs, b_conv_w, b_conv_b, b_filt_w1, b_filt_b1, b_filt_w2, b_filt_b2, b_filt_w3, b_skip,
              q_norm, kv_norm, w_uq, w_uk, w_uv, w_branch_a, w_branch_b, w_branch_c, w_out,
              peer_wq, peer_sub_keys, peer_u, peer_v, final_norm):
    rope = axial_rope_tables(x_sample.shape[1], x_sample.dtype)
    ctx_cond = c_ctx[None, :]
    xp, xs = x_prompt, x_sample
    new_ckv, new_kpe = [], []
    for l in range(DEPTH):
        lp = {
            'w_ada': w_ada[l], 'b_ada': b_ada[l], 'norm1': norm1[l], 'norm2': norm2[l], 'w_in': w_in[l],
            'a_ws': a_ws[l], 'a_bs': a_bs[l], 'b_conv_w': b_conv_w[l], 'b_conv_b': b_conv_b[l],
            'b_filt_w1': b_filt_w1[l], 'b_filt_b1': b_filt_b1[l], 'b_filt_w2': b_filt_w2[l],
            'b_filt_b2': b_filt_b2[l], 'b_filt_w3': b_filt_w3[l], 'b_skip': b_skip[l],
            'q_norm': q_norm[l], 'kv_norm': kv_norm[l], 'w_uq': w_uq[l], 'w_uk': w_uk[l], 'w_uv': w_uv[l],
            'w_branch_a': w_branch_a[l], 'w_branch_b': w_branch_b[l], 'w_branch_c': w_branch_c[l],
            'w_out': w_out[l], 'peer_wq': peer_wq[l], 'peer_sub_keys': peer_sub_keys[l],
            'peer_u': peer_u[l], 'peer_v': peer_v[l],
        }
        xp, ckv_l, kpe_l = trunk_layer(xp, ctx_cond, lp, None, None)
        new_ckv.append(ckv_l)
        new_kpe.append(kpe_l)
        xs, _, _ = trunk_layer(xs, c, lp, (cache_ckv[:, l], cache_kpe[:, l]), rope)
    y_prompt = rms_norm(xp, final_norm)
    y_sample = rms_norm(xs, final_norm)
    state_ckv = jnp.stack(new_ckv, axis=1)
    state_kpe = jnp.stack(new_kpe, axis=1)
    return (y_prompt, y_sample, state_ckv, state_kpe)


_drawn_inputs = setup_inputs


def setup_inputs(seed=0):
    import zlib

    import numpy as np

    out = dict(_drawn_inputs(seed))
    spreads = {}
    factors = {'cache_ckv': 6.235,
     'cache_kpe': 8.0,
     'norm1': 2.947,
     'norm2': 14.536,
     'a_bs': 8.0,
     'b_conv_b': 8.0,
     'b_filt_b1': 8.0,
     'b_filt_b2': 8.0,
     'q_norm': 8.0,
     'kv_norm': 8.954,
     'final_norm': 7.995}
    for name, (base, spread) in spreads.items():
        noise = np.random.default_rng([zlib.crc32(name.encode()), seed]).standard_normal(out[name].shape)
        drawn = base * np.exp(spread * noise) if base else spread * noise
        out[name] = __import__('jax').numpy.asarray(drawn.astype(out[name].dtype))
    for name, factor in factors.items():
        out[name] = (out[name] * factor).astype(out[name].dtype)
    return out
```

```python
from contextlib import ExitStack

import concourse.bass as bass
from concourse import mybir

ALU = mybir.AluOpType
ACT = mybir.ActivationFunctionType
AX = mybir.AxisListType
F32 = mybir.dt.float32
U32 = mybir.dt.uint32

P = 128
D = 1024
KC = D // P
LAYERS = 2
SAMPLE, PROMPT, PAST = 512, 128, 128
T = SAMPLE + PROMPT
TILES = T // P
STILES = SAMPLE // P
EPS = 1e-6
A_W = B_W = 256
HEADS, NOPE, ROPE, VD = 8, 64, 32, 64
Q_RANK, KV_RANK = 256, 128
QH = NOPE + ROPE
SCALE = float(QH) ** -0.5
EMB, HID = 33, 64
PH, TOPK, NKEYS = 8, 16, 128
EXPERTS = PH * TOPK

COL_U = 3 * D
COL_V = COL_U + A_W
COL_B = COL_V + A_W
COL_Q = COL_B + 3 * B_W
COL_KV = COL_Q + Q_RANK
KV_COLS = KV_RANK + ROPE

SLOTS = 4
CW = 256
N_ADA = 6 * D // CW
CH_Q = N_ADA
CH_B = CH_Q + 4
CH_WIN = CH_B + 3
CH_DFT = CH_WIN + 1
CH_GATE = CH_DFT + 4
CH_OUT = CH_GATE + 4 * (D // CW)
CH_PQ = CH_OUT + D // CW
CHUNKS = CH_PQ + PH * 2 * P // CW
assert CHUNKS % SLOTS == 0 and CH_GATE % SLOTS == 0 and CH_PQ % SLOTS == 0

R_ADA, R_N1, R_N2, R_CW, R_CB, R_SK, R_QN, R_B1, R_B2 = 0, 48, 56, 64, 82, 88, 90, 92, 93
R_ALL = 94

C_ID, C_DFT, C_COS, C_SIN, C_PERM, C_WIN, C_Z = 0, 128, 640, 1152, 1664, 1792, 2304
C_IOTA = C_Z + T
C_ALL = C_IOTA + 16

ROWS_U, ROWS_V = 4, 4


def turn_table():
    order = ["params", "turned_a", "turned_b", "ada", "norm1"]
    order += [("token", j) for j in range(TILES)] + [("u", c) for c in range(2)] + [("conv", c) for c in range(6)]
    order += ["mix_a", "hy_turn", "filt1", "filt2", "filt3a", "filt3b"]
    order += [("dft", j) for j in range(TILES)] + [("idft", c) for c in range(2)]
    order += ["at_turn0", "at_turn1"] + [("qn", i) for i in range(4)] + [("qp", i) for i in range(2)] + ["rope"]
    order += [("ql", h) for h in range(HEADS)]
    for h in range(HEADS):
        order += attention_order(h)
    order += [("gate", n) for n in range(3 * KC)] + [("out", n) for n in range(KC)] + ["norm2"]
    order += [("pq", n) for n in range(2 * PH)] + [("key", n) for n in range(2 * TILES)]
    order += [("tok", j) for j in range(TILES)] + [("peer", n) for n in range(2 * TILES)]
    assert len(order) % 2 == 0, len(order)
    return {name: n for n, name in enumerate(order)}


def attention_order(h):
    order = [("S", h, 0)]
    for j in range(1, TILES):
        order += [("S", h, j), ("T", h, j - 1)]
    order += [("T", h, TILES - 1), ("PV", h)]
    if h % 2:
        order.append(("YC", h // 2))
    return order


TURN = turn_table()
TURNS = len(TURN)
FIRST_TURNS = TILES + 1


def turn_value(l, name, more=0):
    return FIRST_TURNS // 2 + l * (TURNS // 2) + TURN[name] // 2 + 1 + more


class Signal:

    def __init__(self, sem, layer, first=0):
        self.sem, self.layer, self.first = sem, layer, first

    def after(self, l, n):
        return self.first + l * self.layer + n


def build(nc, x_prompt, x_sample, cache_ckv, cache_kpe, c, c_ctx, w_ada, b_ada, norm1, norm2, w_in,
          a_ws, a_bs, b_conv_w, b_conv_b, b_filt_w1, b_filt_b1, b_filt_w2, b_filt_b2, b_filt_w3, b_skip,
          q_norm, kv_norm, w_uq, w_uk, w_uv, w_branch_a, w_branch_b, w_branch_c, w_out,
          peer_wq, peer_sub_keys, peer_u, peer_v, final_norm, consts, tables,
          y_prompt, y_sample, state_ckv, state_kpe):
    with ExitStack() as ctx:
        def sb(name, shape, dt=F32):
            return ctx.enter_context(nc.sbuf_tensor(name, shape, dt))

        def sem(name):
            return ctx.enter_context(nc.semaphore(name))

        def signal(name, layer, first=0):
            return Signal(sem(name), layer, first)

        cst = sb("cst", [P, C_ALL])
        ident = cst[:, C_ID:C_ID + P]
        x_t = sb("x_t", [P, KC, T])
        h_t = sb("h_t", [P, KC, T])
        m_t = sb("m_t", [P, KC, T])
        ring = sb("ring", [P, SLOTS, KC * CW])
        mean_w = sb("mean_w", [P, P])
        one_row = sb("one_row", [1, NOPE])
        eps_t = sb("eps_t", [P, 1])
        cond_rows = sb("cond_rows", [3 * KC, P])
        cond_t = sb("cond_t", [P, 3, KC])
        par_rows = sb("par_rows", [R_ALL, P])
        par = sb("par", [P, R_ALL])
        kvn = sb("kvn", [P, KV_RANK])
        abs_row = sb("abs_row", [1, 4, P])
        past = sb("past", [P, 2, P])
        uv = sb("uv", [P, HEADS * VD])
        uq = sb("uq", [P, 2, HEADS * QH])
        f_w1 = sb("f_w1", [EMB, HID])
        f_w2 = sb("f_w2", [HID, HID])
        f_w3 = sb("f_w3", [HID, 2 * B_W])
        turned = sb("turned", [P, 10, P])
        mod = sb("mod", [P, 6 * KC, 2])
        amp = sb("amp", [P, 2, KC, 2])
        root = sb("root", [P, T])
        rinv = root
        u_t = sb("u_t", [P, 2, T])
        cv = sb("cv", [P, 6, T])
        zc = sb("zc", [P, TILES, 512])
        ss = sb("ss", [P, 2, TILES])
        sr = sb("sr", [P, 2, TILES])
        kt = sb("kt", [P, 2, T + PAST])
        stat = sb("stat", [P, 2, 4])
        g2_all = sb("g2_all", [P, TILES, KC])
        g2_cur = sb("g2_cur", [P, KC])
        table_base = sb("table_base", [P, 1])
        ARENA = 10368
        arena = sb("arena", [P, ARENA])

        def view(start, *dims):
            n = 1
            for d in dims:
                n *= d
            assert start + n <= ARENA
            flat = arena[:, start:start + n]
            if len(dims) == 1:
                return flat
            names = " ".join("abc"[:len(dims)])
            return flat.rearrange(f"p ({names}) -> p {names}", **dict(zip("abc", dims)))

        ws_in = view(0, 6, P)
        uk_in = view(6 * P, HEADS * NOPE)
        hy = view(0, TILES, 3 * B_W)
        y_f = view(3840, TILES, 2 * B_W)
        tmp_f = view(6400, TILES, B_W)
        hid = view(7680, 2, T)
        v_tok = view(8960, TILES, A_W)
        spec = m_t[:].rearrange("p k t -> p (k t)").rearrange("p (j n) -> p j n", j=TILES)
        qn_t = view(0, 4, T)
        yc_t = qn_t
        zq_t = view(2560, 2, T)
        qp_t = view(3840, 2, T)
        prob = view(5120, 2, T)
        prob_t = view(6400, TILES, SAMPLE)
        prob_tp = view(8960, P)
        ol_t = view(9088, 2, T)
        dump = view(6400, TILES, Q_RANK + KV_RANK)
        rope_tmp = view(6400, 3, SAMPLE)
        ql_t = m_t
        gate_s = view(5120, 2, T)
        gate_y = view(6400, 2, T)
        pq_t = view(0, 2 * PH, T)
        m_flat = m_t[:].rearrange("p k t -> p (k t)")
        cand = m_flat[:, 0:2048]
        repl = m_flat[:, 2048:4096]
        zc_flat = zc[:].rearrange("p j n -> p (j n)")
        top_v = zc_flat[:, 0:256].rearrange("p (h s k) -> p h s k", h=PH, s=2)
        top_i = zc_flat[:, 256:512].bitcast(U32).rearrange("p (h s k) -> p h s k", h=PH, s=2)
        top_f = zc_flat[:, 512:768].rearrange("p (h s k) -> p h s k", h=PH, s=2)
        best_v = zc_flat[:, 768:896].rearrange("p (h k) -> p h k", h=PH)
        best_p = zc_flat[:, 896:1024].bitcast(U32)
        best_a = zc_flat[:, 1024:1280].bitcast(U32).rearrange("p (s n) -> p s n", s=2)
        best_f = zc_flat[:, 1280:1536].rearrange("p (s n) -> p s n", s=2)
        best_i = zc_flat[:, 1536:1792].rearrange("p (s n) -> p s n", s=2)
        best_e = zc_flat[:, 1792:1920].rearrange("p (h k) -> p h k", h=PH)
        best_s = zc_flat[:, 1920:1928]
        best_r = zc_flat[:, 1928:1936]
        kt_flat = kt[:].rearrange("p a n -> p (a n)")
        idx_u, idx_v = kt_flat[:, 0:P].bitcast(U32), kt_flat[:, 4 * P:5 * P].bitcast(U32)
        g_cur = kt_flat[:, P:2 * P]
        dots, acts = kt_flat[:, 2 * P:3 * P], kt_flat[:, 3 * P:4 * P]
        rows_u = view(0, ROWS_U, D)
        rows_v = view(4096, ROWS_V, D)
        cv_flat = cv[:].rearrange("p k t -> p (k t)")
        diag = [view(8192, TOPK, P), cv_flat[:, 0:TOPK * P].rearrange("p (k n) -> p k n", k=TOPK)]
        tok_cur = cv_flat[:, 2048:3072]
        tok_all = m_flat.rearrange("p (j n) -> p j n", j=TILES)
        y_tok = zc_flat[:, 0:D]
        x_rows = view(0, TILES, D) if TILES * D <= ARENA else None
        y_rows = view(0, TILES, D)

        idx_flat, g_flat = u_t[:, 0, :].bitcast(U32), u_t[:, 1, :]

        ps = ctx.enter_context(nc.psum_tensor("ps", [P, 8 * 512], F32))
        accs = [ps[:, 0:1536], ps[:, 1536:3072]]

        def acc(name):
            return accs[TURN[name] % 2]

        acc_full = [sem("acc_full0"), sem("acc_full1")]
        acc_free = [sem("acc_free0"), sem("acc_free1")]
        consts_in, x_in = sem("consts_in"), sem("x_in")
        setup_done = sem("setup_done")
        par_zero = sem("par_zero")
        x_ready = sem("x_ready")
        cond_ready = sem("cond_ready")
        PARAM_DMAS = 27
        params_in = signal("params_in", 16 * PARAM_DMAS)
        w_in_slot = [signal(f"w_slot{s}", 16 * (CHUNKS // SLOTS - (D // CW if s == SLOTS - 1 else 0)))
                     for s in range(SLOTS)]
        branch_in = signal("branch_in", 16 * 3 * (D // CW))
        w_free = signal("w_free", CHUNKS, SLOTS)
        par_ready = signal("par_ready", 1)
        turned_ready = signal("turned_ready", 2)
        mod_ready = signal("mod_ready", 1)
        sq_ready = signal("sq_ready", 2 * KC)
        root_ready = signal("root_ready", 2)
        scaled = signal("scaled", 2 * KC)
        h_ready = signal("h_ready", 2 * KC)
        zc_ready = signal("zc_ready", TILES)
        u_ready = signal("u_ready", 2)
        ya_ready = signal("ya_ready", 1)
        x1v_ready = signal("x1v_ready", 1)
        hyu_ready = signal("hyu_ready", 1)
        arg_ready = signal("arg_ready", 2)
        sin_ready = signal("sin_ready", 2)
        taps_ready = signal("taps_ready", 1)
        spec_ready = signal("spec_ready", TILES)
        yf_ready = signal("yf_ready", 1)
        yb_ready = signal("yb_ready", 1)
        ssr_ready = signal("ssr_ready", 1)
        lat_ready = signal("lat_ready", 1)
        state_out = signal("state_out", 32)
        lat_t_ready = signal("lat_t_ready", 1)
        q_ready = signal("q_ready", 6)
        rope_ready = signal("rope_ready", 1)
        ql_ready = signal("ql_ready", HEADS)
        max_ready = signal("max_ready", HEADS * TILES)
        exp_ready = signal("exp_ready", HEADS * TILES)
        prob_ready = signal("prob_ready", HEADS * TILES)
        probt_ready = signal("probt_ready", HEADS * TILES)
        ol_ready = signal("ol_ready", HEADS)
        yc_ready = signal("yc_ready", HEADS // 2)
        sig_ready = signal("sig_ready", 3 * KC)
        merged_credit = signal("merged_credit", 3 * KC + 2)
        merged_ready = signal("merged_ready", 3 * KC)
        xmix_ready = signal("xmix_ready", KC)
        pq_ready = signal("pq_ready", 2 * PH)
        soft_in = signal("soft_in", TILES)
        soft_exp = signal("soft_exp", TILES)
        sel_ready = signal("sel_ready", TILES)
        tok_ready = signal("tok_ready", TILES)
        tokc_ready = signal("tokc_ready", TILES)
        rows_u_in = [signal(f"rows_u_in{s}", 16 * TILES * EXPERTS // ROWS_U) for s in range(ROWS_U)]
        rows_v_in = [signal(f"rows_v_in{s}", 16 * TILES * EXPERTS // ROWS_V) for s in range(ROWS_V)]
        rows_u_free = signal("rows_u_free", TILES * EXPERTS, ROWS_U)
        rows_v_free = signal("rows_v_free", TILES * EXPERTS, ROWS_V)
        dots_ready = signal("dots_ready", TILES * PH)
        acts_ready = signal("acts_ready", TILES * PH)
        diag_ready = signal("diag_ready", TILES * PH)
        ytok_ready = signal("ytok_ready", TILES)
        x_done = signal("x_done", TILES)
        fin_ready = sem("fin_ready")
        yrow_ready = sem("yrow_ready")
        y_out = sem("y_out")

        passed = {"pe": sem("passed_pe"), "dve": sem("passed_dve"), "pool": sem("passed_pool")}

        def carry_waits(eng, name):
            eng.sem_inc(passed[name], 1)

        block = ctx.enter_context(nc.Block())

        @block.sync
        def _(sp):
            sp.dma_start(cst[:], consts).then_inc(consts_in, 16)
            sp.dma_start(cond_rows[0:KC, :], c.rearrange("a (k p) -> (a k) p", p=P)).then_inc(x_in, 16)
            sp.dma_start(cond_rows[KC:2 * KC, :], c_ctx.rearrange("(k p) -> k p", p=P)).then_inc(x_in, 16)
            sp.dma_start(cond_rows[2 * KC:, :], final_norm.rearrange("(k p) -> k p", p=P)).then_inc(x_in, 16)
            sp.dma_start(x_rows[:, 0:STILES, :], x_sample[0].rearrange("(j p) d -> p j d", p=P)).then_inc(x_in, 16)
            sp.dma_start(x_rows[:, STILES, :], x_prompt[0]).then_inc(x_in, 16)

            def load(l, n, src, more=0):
                slot = n % SLOTS
                k, cols = src.shape[1], src.shape[2]
                sp.wait_ge(w_free.sem, l * CHUNKS + n + more + 1)
                sp.dma_start(ring[:, slot, 0:k * cols].rearrange("p (k n) -> p k n", k=k), src)\
                    .then_inc(w_in_slot[slot].sem, 16)

            def cols_of(w, l, start, n=CW):
                return w[l, :, bass.ds(start, n)].rearrange("(k p) n -> p k n", p=P)

            with sp.Fori(0, LAYERS) as l:
                with sp.Fori(0, N_ADA // SLOTS) as i:
                    for s in range(SLOTS):
                        load(l, s, cols_of(w_ada, l, (i * SLOTS + s) * CW), i * SLOTS)
                load(l, CH_Q, cols_of(w_in, l, COL_Q))
                load(l, CH_Q + 1, cols_of(w_in, l, COL_KV, KV_COLS))
                load(l, CH_Q + 2, cols_of(w_in, l, COL_V))
                load(l, CH_Q + 3, cols_of(w_in, l, COL_U))
                for s in range(3):
                    load(l, CH_B + s, cols_of(w_in, l, COL_B + s * CW))
                for s in range(5):
                    load(l, CH_WIN + s, tables[s].rearrange("p (j n) -> p j n", j=STILES))
                with sp.Fori(0, D // CW) as i:
                    for s in range(3):
                        load(l, CH_GATE + s, cols_of(w_in, l, s * D + i * CW), i * SLOTS)
                    sp.wait_ge(w_free.sem, l * CHUNKS + CH_GATE + 3 + i * SLOTS + 1)
                    stack = ring[:, 3, :].rearrange("p (k n) -> p k n", k=KC)
                    k0 = 0
                    for w in (w_branch_a, w_branch_b, w_branch_c):
                        k = w.shape[1] // P
                        sp.dma_start(stack[:, k0:k0 + k, :], cols_of(w, l, i * CW)).then_inc(branch_in.sem, 16)
                        k0 += k
                for s in range(D // CW):
                    load(l, CH_OUT + s, cols_of(w_out, l, s * CW))
                with sp.Fori(0, 2) as i:
                    for s in range(SLOTS):
                        load(l, CH_PQ + s, cols_of(peer_wq, l, (i * SLOTS + s) * CW), i * SLOTS)
            for j in range(TILES):
                sp.wait_ge(yrow_ready, j + 1)
                dst = y_sample[0, j * P:(j + 1) * P, :] if j < STILES else y_prompt[0]
                sp.dma_start(dst, y_rows[:, j, :]).then_inc(y_out, 16)
            sp.wait_ge(y_out, 16 * TILES)

        @block.tensor
        def _(pe):
            def open_turn(l, name, more=0):
                pe.wait_ge(acc_free[TURN[name] % 2], turn_value(l, name, more))
                return acc(name)

            def close_turn(name, mm):
                mm.then_inc(acc_full[TURN[name] % 2], 1)

            def release(n):
                pe.drain().then_inc(w_free.sem, n)

            def chunk_arrived(l, n, more=0):
                slot, m = n % SLOTS, n // SLOTS + 1
                if slot == SLOTS - 1 and n >= CH_OUT:
                    m -= D // CW
                pe.wait_ge(w_in_slot[slot].sem, w_in_slot[slot].after(l, 16 * m) + 16 * more)
                return ring[:, slot, :].rearrange("p (k n) -> p k n", k=KC)

            def product(a, lhs, rhs, start=True, stop=True):
                n = len(lhs)
                for lo, hi in ((0, SAMPLE), (SAMPLE, T)):
                    for k in range(n):
                        mm = pe.matmul(a[:, lo:hi], lhs[k], rhs[k][:, lo:hi],
                                       start=start and k == 0, stop=stop and k == n - 1)
                return mm

            def blocks(w, c0):
                return [w[:, k, c0:c0 + P] for k in range(KC)]

            h_k = [h_t[:, k, :] for k in range(KC)]

            pe.sem_inc(acc_free[0], 1)
            pe.sem_inc(acc_free[1], 1)
            pe.sem_inc(w_free.sem, SLOTS)
            pe.wait_ge(consts_in, 16)
            pe.wait_ge(x_in, 5 * 16)
            for g in range(TILES):
                pe.wait_ge(acc_free[g % 2], g // 2 + 1)
                for k in range(KC):
                    mm = pe.transpose(accs[g % 2][:, k * P:(k + 1) * P], x_rows[:, g, k * P:(k + 1) * P], ident)
                mm.then_inc(acc_full[g % 2], 1)
            pe.wait_ge(acc_free[TILES % 2], TILES // 2 + 1)
            pe.transpose(accs[TILES % 2][:, 0:3 * KC], cond_rows[:, :], ident[0:3 * KC, 0:3 * KC])\
                .then_inc(acc_full[TILES % 2], 1)

            def root_mean(l, name, first):
                a = open_turn(l, name)
                for lo, hi in ((0, SAMPLE), (SAMPLE, T)):
                    for k in range(KC):
                        if lo == 0:
                            pe.wait_ge(sq_ready.sem, sq_ready.after(l, first + k + 1))
                        mm = pe.matmul(a[:, lo:hi], mean_w[:], m_t[:, k, lo:hi], start=k == 0, stop=k == KC - 1)
                close_turn(name, mm)

            with pe.Fori(0, LAYERS) as l:
                pe.wait_ge(params_in.sem, params_in.after(l, 16 * PARAM_DMAS))
                a = open_turn(l, "params")
                close_turn("params", pe.transpose(a[:, 0:R_ALL], par_rows[:, :], ident[0:R_ALL, 0:R_ALL]))
                a = open_turn(l, "turned_a")
                for n in range(6):
                    mm = pe.transpose(a[:, n * P:(n + 1) * P], ws_in[:, n, :], ident)
                close_turn("turned_a", mm)
                a = open_turn(l, "turned_b")
                for n in range(4):
                    pe.transpose(a[:, n * P:(n + 1) * P], uk_in[:, n * P:(n + 1) * P], ident)
                for n in range(2):
                    mm = pe.transpose(a[:, (4 + n) * P:(5 + n) * P], past[:, n, :], ident)
                close_turn("turned_b", mm)

                a = open_turn(l, "ada")
                pe.wait_ge(cond_ready, 2)
                carry_waits(pe, "pe")
                with pe.Fori(0, N_ADA // SLOTS) as i:
                    for s in range(SLOTS):
                        w = chunk_arrived(l, s, i)
                        for half in range(2):
                            at = a[:, bass.ds((i * SLOTS + s) * 4 + half * 2, 2)]
                            for k in range(KC):
                                mm = pe.matmul(at, w[:, k, half * P:(half + 1) * P], cond_t[:, 0:2, k],
                                               start=k == 0, stop=k == KC - 1)
                        release(1)
                pe.drain().then_inc(acc_full[TURN["ada"] % 2], 1)
                root_mean(l, "norm1", 0)
                pe.wait_ge(h_ready.sem, h_ready.after(l, KC))

                wq, wkv, wv, wu = (chunk_arrived(l, CH_Q + s) for s in range(4))
                wkv = ring[:, 1, 0:KC * KV_COLS].rearrange("p (k n) -> p k n", k=KC)
                for j in range(TILES):
                    a = open_turn(l, ("token", j))
                    for at, w, n in ((0, wq, Q_RANK), (Q_RANK, wkv, KV_COLS), (512, wv, A_W)):
                        for k in range(KC):
                            mm = pe.matmul(a[:, at:at + n], h_t[:, k, j * P:(j + 1) * P], w[:, k, 0:n],
                                           start=k == 0, stop=k == KC - 1)
                    close_turn(("token", j), mm)
                release(3)
                for c in range(2):
                    a = open_turn(l, ("u", c))
                    mm = product(a, blocks(wu, c * P), h_k)
                    close_turn(("u", c), mm)
                release(1)
                for c in range(6):
                    a = open_turn(l, ("conv", c))
                    w = chunk_arrived(l, CH_B + c // 2)
                    mm = product(a, blocks(w, c % 2 * P), h_k)
                    close_turn(("conv", c), mm)
                    if c % 2:
                        release(1)

                a = open_turn(l, "mix_a")
                pe.wait_ge(zc_ready.sem, zc_ready.after(l, TILES))
                pe.wait_ge(turned_ready.sem, turned_ready.after(l, 2))
                for c in range(2):
                    for j in range(TILES):
                        at = (c * TILES + j) * P
                        for g in (2 * c, 2 * c + 1):
                            out = a[(g % 2) * 64:(g % 2) * 64 + 64, at:at + P]
                            pe.matmul(out, v_tok[:, j, g * 64:(g + 1) * 64], turned[:, g, :], start=True, stop=False)
                            mm = pe.matmul(out, one_row[:, :], abs_row[:, g, :], start=False, stop=True)
                close_turn("mix_a", mm)

                a = open_turn(l, "hy_turn")
                pe.wait_ge(x1v_ready.sem, x1v_ready.after(l, 1))
                for j in range(TILES):
                    for c in range(2):
                        at = (j * 2 + c) * P
                        mm = pe.transpose(a[:, at:at + P], cv[:, 2 + c, j * P:(j + 1) * P], ident)
                close_turn("hy_turn", mm)
                a = open_turn(l, "filt1")
                carry_waits(pe, "pe")
                mm = product(a[0:HID], [f_w1[:, :]], [cst[0:EMB, C_Z:C_Z + T]])
                close_turn("filt1", mm)
                a = open_turn(l, "filt2")
                pe.wait_ge(sin_ready.sem, sin_ready.after(l, 1))
                carry_waits(pe, "pe")
                mm = product(a[0:HID], [f_w2[:, :]], [hid[0:HID, 0, :]])
                close_turn("filt2", mm)
                for name, tiles in (("filt3a", (0, 1, 2)), ("filt3b", (3, 4))):
                    a = open_turn(l, name)
                    pe.wait_ge(sin_ready.sem, sin_ready.after(l, 2))
                    for n, j in enumerate(tiles):
                        mm = pe.matmul(a[:, n * 512:(n + 1) * 512], hid[0:HID, 1, j * P:(j + 1) * P], f_w3[:, :],
                                       start=True, stop=True)
                    close_turn(name, mm)
                pe.wait_ge(taps_ready.sem, taps_ready.after(l, 1))
                pe.wait_ge(hyu_ready.sem, hyu_ready.after(l, 1))
                carry_waits(pe, "pe")
                pe.drain().then_inc(w_free.sem, 1)
                cos, sin, icos, isin = (chunk_arrived(l, CH_DFT + s).rearrange("p k n -> p (k n)")
                                        .rearrange("p (j n) -> p j n", j=STILES) for s in range(4))
                for q in range(TILES):
                    a = open_turn(l, ("dft", q))
                    for at, lo, big, small in ((0, 0, cos, 0), (512, B_W, sin, 1)):
                        if q < STILES:
                            for j in range(STILES):
                                mm = pe.matmul(a[:, at:at + 512], big[:, j, q * P:(q + 1) * P], hy[:, j, lo:lo + 512],
                                               start=j == 0, stop=j == STILES - 1)
                        else:
                            w = cst[:, C_DFT + small * P:C_DFT + (small + 1) * P]
                            mm = pe.matmul(a[:, at:at + 512], w, hy[:, STILES, lo:lo + 512], start=True, stop=True)
                    close_turn(("dft", q), mm)
                    if q == STILES - 1:
                        release(2)
                pe.wait_ge(yf_ready.sem, yf_ready.after(l, 1))
                for c in range(2):
                    a = open_turn(l, ("idft", c))
                    for n, (m, at) in enumerate([(m, at) for m in range(STILES) for at in (0, B_W)]):
                        w = icos if at == 0 else isin
                        pe.matmul(a[:, 0:SAMPLE], y_f[:, m, at + c * P:at + (c + 1) * P], w[:, m, :],
                                  start=n == 0, stop=n == 2 * STILES - 1)
                    for n, at in enumerate((0, B_W)):
                        w = cst[:, C_DFT + (2 + n) * P:C_DFT + (3 + n) * P]
                        mm = pe.matmul(a[:, SAMPLE:T], y_f[:, STILES, at + c * P:at + (c + 1) * P], w,
                                       start=n == 0, stop=n == 1)
                    close_turn(("idft", c), mm)
                release(2)

                pe.wait_ge(lat_ready.sem, lat_ready.after(l, 1))
                for name, tiles in (("at_turn0", (0, 1, 2)), ("at_turn1", (3, 4))):
                    a = open_turn(l, name)
                    for n, j in enumerate(tiles):
                        for b in range(4):
                            mm = pe.transpose(a[:, n * 512 + b * P:n * 512 + (b + 1) * P],
                                              zc[:, j, b * P:(b + 1) * P], ident)
                    close_turn(name, mm)
                pe.wait_ge(lat_t_ready.sem, lat_t_ready.after(l, 1))
                zq_k = [zq_t[:, k, :] for k in range(2)]
                for i in range(4):
                    a = open_turn(l, ("qn", i))
                    close_turn(("qn", i), product(a, [uq[:, k, i * P:(i + 1) * P] for k in range(2)], zq_k))
                for i in range(2):
                    a = open_turn(l, ("qp", i))
                    close_turn(("qp", i), product(a, [uq[:, k, (4 + i) * P:(5 + i) * P] for k in range(2)], zq_k))
                a = open_turn(l, "rope")
                pe.wait_ge(q_ready.sem, q_ready.after(l, 6))
                perm = cst[:, C_PERM:C_PERM + P]
                for n, src in enumerate((qp_t[:, 0, 0:SAMPLE], qp_t[:, 1, 0:SAMPLE], kt[:, 1, 0:SAMPLE])):
                    mm = pe.matmul(a[:, n * 512:(n + 1) * 512], perm, src, start=True, stop=True)
                close_turn("rope", mm)
                for h in range(HEADS):
                    a = open_turn(l, ("ql", h))
                    lo = h % 2 * NOPE
                    close_turn(("ql", h), product(a, [turned[lo:lo + NOPE, 6 + h // 2, :]],
                                                  [qn_t[lo:lo + NOPE, h // 2, :]]))
                pe.wait_ge(rope_ready.sem, rope_ready.after(l, 1))
                pe.wait_ge(ql_ready.sem, ql_ready.after(l, HEADS))

                def scores(h, j):
                    a = open_turn(l, ("S", h, j))
                    r = h % 4 * ROPE
                    tile = slice(j * P, (j + 1) * P)
                    keys = ((0, 0, SAMPLE), (SAMPLE, T, T + PAST)) if j < STILES else ((0, SAMPLE, T),)
                    for at, lo, hi in keys:
                        pe.matmul(a[:, at:at + hi - lo], ql_t[:, h, tile], kt[:, 0, lo:hi], start=True, stop=False)
                        mm = pe.matmul(a[:, at:at + hi - lo], qp_t[r:r + ROPE, h // 4, tile], kt[r:r + ROPE, 1, lo:hi],
                                       start=False, stop=True)
                    close_turn(("S", h, j), mm)

                def turn_probs(h, j):
                    a = open_turn(l, ("T", h, j))
                    pe.wait_ge(prob_ready.sem, prob_ready.after(l, h * TILES + j + 1))
                    for b in range(TILES if j < STILES else 1):
                        mm = pe.transpose(a[:, b * P:(b + 1) * P], prob[:, (h * TILES + j) % 2, b * P:(b + 1) * P],
                                          ident)
                    close_turn(("T", h, j), mm)

                def values(h):
                    a = open_turn(l, ("PV", h))
                    pe.wait_ge(probt_ready.sem, probt_ready.after(l, (h + 1) * TILES))
                    for b in range(TILES):
                        w = zc[:, b, Q_RANK:Q_RANK + KV_RANK] if b < STILES else past[:, 0, :]
                        pe.matmul(a[:, 0:SAMPLE], w, prob_t[:, b, :], start=b == 0, stop=b == TILES - 1)
                    mm = pe.matmul(a[:, SAMPLE:T], zc[:, STILES, Q_RANK:Q_RANK + KV_RANK], prob_tp[:, :],
                                   start=True, stop=True)
                    close_turn(("PV", h), mm)

                def head_out(i):
                    a = open_turn(l, ("YC", i))
                    for h in (2 * i, 2 * i + 1):
                        pe.wait_ge(ol_ready.sem, ol_ready.after(l, h + 1))
                        lo = h % 2 * VD
                        mm = product(a[lo:lo + VD], [uv[:, h * VD:(h + 1) * VD]], [ol_t[:, h % 2, :]])
                    close_turn(("YC", i), mm)

                for h in range(HEADS):
                    for name in attention_order(h):
                        {"S": lambda: scores(*name[1:]), "T": lambda: turn_probs(*name[1:]),
                         "PV": lambda: values(h), "YC": lambda: head_out(h // 2)}[name[0]]()
                pe.wait_ge(yc_ready.sem, yc_ready.after(l, HEADS // 2))
                pe.wait_ge(ya_ready.sem, ya_ready.after(l, 1))
                pe.wait_ge(yb_ready.sem, yb_ready.after(l, 1))

                y_k = [[u_t[:, k, :] for k in range(2)], [cv[:, 2 + k, :] for k in range(2)],
                       [yc_t[:, k, :] for k in range(4)]]
                carry_waits(pe, "pe")
                with pe.Fori(0, D // CW) as i:
                    for b in range(3):
                        wg = chunk_arrived(l, CH_GATE + b, i)
                        if b == 0:
                            pe.wait_ge(branch_in.sem, branch_in.after(l, 48) + i * 48)
                        wb = ring[:, 3, :].rearrange("p (k n) -> p k n", k=KC)
                        for half in range(2):
                            name = ("gate", 2 * b + half)
                            a = open_turn(l, name, i * 3)
                            cols = slice(half * P, (half + 1) * P)
                            for lo, hi, at_g, at_y in ((0, SAMPLE, 0, 512), (SAMPLE, T, 1024, 1024 + P)):
                                for k in range(KC):
                                    pe.matmul(a[:, at_g:at_g + hi - lo], wg[:, k, cols], h_t[:, k, lo:hi],
                                              start=k == 0, stop=k == KC - 1)
                                n = len(y_k[b])
                                for k in range(n):
                                    mm = pe.matmul(a[:, at_y:at_y + hi - lo], wb[:, (0, 2, 4)[b] + k, cols],
                                                   y_k[b][k][:, lo:hi], start=k == 0, stop=k == n - 1)
                            close_turn(name, mm)
                        release(2 if b == 2 else 1)
                pe.wait_ge(merged_ready.sem, merged_ready.after(l, 3 * KC))
                for n in range(KC):
                    a = open_turn(l, ("out", n))
                    w = chunk_arrived(l, CH_OUT + n // 2)
                    mm = product(a, blocks(w, n % 2 * P), [m_t[:, k, :] for k in range(KC)])
                    close_turn(("out", n), mm)
                    if n % 2:
                        release(1)

                root_mean(l, "norm2", KC)
                pe.wait_ge(h_ready.sem, h_ready.after(l, 2 * KC))
                carry_waits(pe, "pe")
                with pe.Fori(0, 2) as i:
                    for s in range(SLOTS):
                        w = chunk_arrived(l, CH_PQ + s, i)
                        for half in range(2):
                            name = ("pq", 2 * s + half)
                            a = open_turn(l, name, i * 4)
                            mm = product(a, blocks(w, half * P), h_k)
                            close_turn(name, mm)
                        release(1)
                pe.wait_ge(pq_ready.sem, pq_ready.after(l, 2 * PH))
                for n in range(2 * TILES):
                    a = open_turn(l, ("key", n))
                    for g in range(PH):
                        hs = n % 2 * PH + g
                        mm = pe.matmul(a[:, g * P:(g + 1) * P], pq_t[:, hs, n // 2 * P:(n // 2 + 1) * P],
                                       turned[:, 4 + g % 2, :], start=True, stop=True)
                    close_turn(("key", n), mm)
                for j in range(TILES):
                    a = open_turn(l, ("tok", j))
                    for k in range(KC):
                        mm = pe.transpose(a[:, k * P:(k + 1) * P], h_t[:, k, j * P:(j + 1) * P], ident)
                    close_turn(("tok", j), mm)

                with pe.Fori(0, TILES) as j:
                    a = open_turn(l, ("peer", 0), j)
                    for h in range(PH):
                        pe.wait_ge(diag_ready.sem, diag_ready.after(l, h + 1) + j * PH)
                        for k in range(TOPK):
                            n = h * TOPK + k
                            s = n % ROWS_V
                            pe.wait_ge(rows_v_in[s].sem,
                                       rows_v_in[s].after(l, 16 * (n // ROWS_V + 1)) + j * (16 * EXPERTS // ROWS_V))
                            for half in range(2):
                                cols = slice(half * 512, (half + 1) * 512)
                                mm = pe.matmul(a[:, cols], diag[h % 2][:, k, :], rows_v[:, s, cols],
                                               start=n == 0, stop=n == EXPERTS - 1)
                            mm.then_inc(rows_v_free.sem, 1)
                    pe.drain().then_inc(acc_full[TURN[("peer", 0)] % 2], 1)
                    a = open_turn(l, ("peer", 1), j)
                    pe.wait_ge(ytok_ready.sem, ytok_ready.after(l, 1) + j)
                    for k in range(KC):
                        mm = pe.transpose(a[:, k * P:(k + 1) * P], y_tok[:, k * P:(k + 1) * P], ident)
                    close_turn(("peer", 1), mm)

            last = FIRST_TURNS + LAYERS * TURNS
            pe.wait_ge(acc_free[last % 2], last // 2 + 1)
            for lo, hi in ((0, SAMPLE), (SAMPLE, T)):
                for k in range(KC):
                    pe.wait_ge(sq_ready.sem, sq_ready.after(LAYERS, k + 1))
                    mm = pe.matmul(accs[last % 2][:, lo:hi], mean_w[:], m_t[:, k, lo:hi], start=k == 0, stop=k == KC - 1)
            mm.then_inc(acc_full[last % 2], 1)
            pe.wait_ge(fin_ready, 1)
            for j in range(TILES):
                g = last + 1 + j
                pe.wait_ge(acc_free[g % 2], g // 2 + 1)
                for k in range(KC):
                    mm = pe.transpose(accs[g % 2][:, k * P:(k + 1) * P], h_t[:, k, j * P:(j + 1) * P], ident)
                mm.then_inc(acc_full[g % 2], 1)

        @block.scalar
        def _(act):
            def full(l, name, more=0):
                act.wait_ge(acc_full[TURN[name] % 2], turn_value(l, name, more))
                return acc(name)

            def give_back(name):
                return acc_free[TURN[name] % 2]

            g = TILES
            act.wait_ge(acc_full[g % 2], g // 2 + 1)
            flat = cond_t[:].rearrange("p a k -> p (a k)")
            act.activation(flat[:, 0:2 * KC], accs[g % 2][:, 0:2 * KC], ACT.Silu).then_inc(cond_ready, 1)
            act.copy(flat[:, 2 * KC:], accs[g % 2][:, 2 * KC:3 * KC]).then_inc(cond_ready, 1)
            act.wait_ge(cond_ready, 2)
            act.sem_inc(acc_free[g % 2], 1)
            act.wait_ge(par_zero, 1)
            act.wait_ge(setup_done, 4)
            act.wait_ge(x_ready, TILES)

            def squares(l, first):
                for k in range(KC):
                    act.activation(m_t[:, k, :], x_t[:, k, :], ACT.Square).then_inc(sq_ready.sem, 1)

            def norm_root(l, name, first):
                a = full(l, name)
                act.activation(root[:, :], a[:, 0:T], ACT.Sqrt, bias=eps_t[:, :]).then_inc(root_ready.sem, 1)
                act.wait_ge(root_ready.sem, root_ready.after(l, first + 1))
                act.sem_inc(give_back(name), 1)

            def add_shift(l, first, shift):
                for k in range(KC):
                    act.wait_ge(scaled.sem, scaled.after(l, first + k + 1))
                    act.activation(h_t[:, k, 0:SAMPLE], h_t[:, k, 0:SAMPLE], ACT.Identity,
                                   bias=mod[:, shift + k, 0:1])
                    act.activation(h_t[:, k, SAMPLE:T], h_t[:, k, SAMPLE:T], ACT.Identity,
                                   bias=mod[:, shift + k, 1:2]).then_inc(h_ready.sem, 1)

            with act.Fori(0, LAYERS) as l:
                def put(dst, src):
                    act.dma_start(dst, src).then_inc(params_in.sem, 16)

                def as_rows(v):
                    return v.rearrange("(k p) -> k p", p=P)

                put(par_rows[R_ADA:R_N1, :], as_rows(b_ada[l]))
                put(par_rows[R_N1:R_N2, :], as_rows(norm1[l]))
                put(par_rows[R_N2:R_CW, :], as_rows(norm2[l]))
                put(par_rows[R_CW:R_CB, :], b_conv_w[l].rearrange("w (k p) -> (w k) p", p=P))
                put(par_rows[R_CB:R_SK, :], as_rows(b_conv_b[l]))
                put(par_rows[R_SK:R_QN, :], as_rows(b_skip[l]))
                put(par_rows[R_QN:R_B1, :], as_rows(q_norm[l]))
                put(par_rows[R_B1:R_B2, 0:HID], b_filt_b1[bass.ds(l, 1), :])
                put(par_rows[R_B2:R_ALL, 0:HID], b_filt_b2[bass.ds(l, 1), :])
                put(kvn[:, :], kv_norm[bass.ds(l, 1), :].to_broadcast([P, KV_RANK]))
                put(abs_row[:, :, :], a_bs[bass.ds(l, 1)])
                put(ws_in[:, 0:4, :], a_ws[l].rearrange("g p q -> p g q"))
                put(ws_in[:, 4:6, :], peer_sub_keys[l].rearrange("s n k -> n s k"))
                put(uk_in[:, :], w_uk[l].rearrange("c h n -> c (h n)"))
                put(past[:, 0, :], cache_ckv[0, l])
                for r in range(4):
                    put(past[:, 1, r * ROPE:(r + 1) * ROPE], cache_kpe[0, l])
                put(uv[:, :], w_uv[l].rearrange("c h n -> c (h n)"))
                for k in range(2):
                    heads = w_uq[l, k * P:(k + 1) * P, :].rearrange("p (h n) -> p h n", h=HEADS)
                    put(uq[:, k, 0:HEADS * NOPE].rearrange("p (h n) -> p h n", h=HEADS), heads[:, :, 0:NOPE])
                    put(uq[:, k, HEADS * NOPE:].rearrange("p (h n) -> p h n", h=HEADS), heads[:, :, NOPE:QH])
                put(f_w1[:, :], b_filt_w1[l])
                put(f_w2[:, :], b_filt_w2[l])
                put(f_w3[:, :], b_filt_w3[l])
                squares(l, 0)
                norm_root(l, "norm1", 0)
                act.wait_ge(mod_ready.sem, mod_ready.after(l, 1))
                add_shift(l, 0, 0)

                for j in range(TILES):
                    a = full(l, ("token", j))
                    act.activation(v_tok[:, j, :], a[:, 512:512 + A_W], ACT.Gelu_apprx_tanh)
                    act.copy(zc[:, j, 0:Q_RANK + KV_RANK], a[:, 0:Q_RANK + KV_RANK])
                    act.copy(zc[:, j, Q_RANK + KV_RANK:512].rearrange("p (a b) -> p a b", a=4),
                             a[:, None, Q_RANK + KV_RANK:Q_RANK + KV_COLS].to_broadcast([P, 4, ROPE]))
                    act.activation(dump[:, j, 0:Q_RANK], a[:, 0:Q_RANK], ACT.Square, accum_out=ss[:, 0, j:j + 1])
                    act.activation(dump[:, j, Q_RANK:], a[:, Q_RANK:Q_RANK + KV_RANK], ACT.Square,
                                   accum_out=ss[:, 1, j:j + 1]).then_inc(zc_ready.sem, 1)
                    act.wait_ge(zc_ready.sem, zc_ready.after(l, j + 1))
                    act.sem_inc(give_back(("token", j)), 1)
                for n, width in enumerate((Q_RANK, KV_RANK)):
                    last = act.activation(sr[:, n, :], ss[:, n, :], ACT.Sqrt, bias=eps_t[:, :], scale=1.0 / width)
                last.then_inc(ssr_ready.sem, 1)
                for c in range(2):
                    a = full(l, ("u", c))
                    act.activation(u_t[:, c, :], a[:, 0:T], ACT.Gelu_apprx_tanh).then_inc(u_ready.sem, 1)
                    act.wait_ge(u_ready.sem, u_ready.after(l, c + 1))
                    act.sem_inc(give_back(("u", c)), 1)

                a = full(l, "hy_turn")
                act.copy(hy[:, :, B_W:2 * B_W], a[:, 0:TILES * B_W].rearrange("p (j n) -> p j n", j=TILES))\
                    .then_inc(hyu_ready.sem, 1)
                act.wait_ge(hyu_ready.sem, hyu_ready.after(l, 1))
                act.sem_inc(give_back("hy_turn"), 1)
                for n in range(2):
                    act.wait_ge(arg_ready.sem, arg_ready.after(l, n + 1))
                    act.activation(hid[0:HID, n, :], hid[0:HID, n, :], ACT.Sin).then_inc(sin_ready.sem, 1)
                for q in range(TILES):
                    a = full(l, ("dft", q))
                    act.copy(spec[:, q, :], a[:, 0:1024]).then_inc(spec_ready.sem, 1)
                    act.wait_ge(spec_ready.sem, spec_ready.after(l, q + 1))
                    act.sem_inc(give_back(("dft", q)), 1)

                act.wait_ge(lat_ready.sem, lat_ready.after(l, 1))
                act.dma_start(state_ckv[0, l], zc[:, STILES, Q_RANK:Q_RANK + KV_RANK]).then_inc(state_out.sem, 16)
                act.dma_start(state_kpe[0, l], zc[:, STILES, 384:384 + ROPE]).then_inc(state_out.sem, 16)
                for n in range(6):
                    name = ("qn", n) if n < 4 else ("qp", n - 4)
                    a = full(l, name)
                    act.copy(qn_t[:, n, :] if n < 4 else qp_t[:, n - 4, :], a[:, 0:T]).then_inc(q_ready.sem, 1)
                    act.wait_ge(q_ready.sem, q_ready.after(l, n + 1))
                    act.sem_inc(give_back(name), 1)
                for h in range(HEADS):
                    a = full(l, ("ql", h))
                    act.copy(ql_t[:, h, :], a[:, 0:T]).then_inc(ql_ready.sem, 1)
                    act.wait_ge(ql_ready.sem, ql_ready.after(l, h + 1))
                    act.sem_inc(give_back(("ql", h)), 1)

                def exps(h, j):
                    m, width = h * TILES + j, T if j < STILES else P
                    a = full(l, ("S", h, j))
                    act.wait_ge(max_ready.sem, max_ready.after(l, m + 1))
                    act.activation(prob[:, m % 2, 0:width], a[:, 0:width], ACT.Exp, bias=stat[:, m % 2, 1:2],
                                   scale=SCALE, accum_out=stat[:, m % 2, 2:3]).then_inc(exp_ready.sem, 1)
                    act.wait_ge(exp_ready.sem, exp_ready.after(l, m + 1))
                    act.sem_inc(give_back(("S", h, j)), 1)

                def take_turned(h, j):
                    m = h * TILES + j
                    a = full(l, ("T", h, j))
                    if j < STILES:
                        act.copy(prob_t[:, :, j * P:(j + 1) * P], a[:, 0:T].rearrange("p (b n) -> p b n", b=TILES))\
                            .then_inc(probt_ready.sem, 1)
                    else:
                        act.copy(prob_tp[:, :], a[:, 0:P]).then_inc(probt_ready.sem, 1)
                    act.wait_ge(probt_ready.sem, probt_ready.after(l, m + 1))
                    act.sem_inc(give_back(("T", h, j)), 1)

                def take_values(h):
                    a = full(l, ("PV", h))
                    act.copy(ol_t[:, h % 2, :], a[:, 0:T]).then_inc(ol_ready.sem, 1)
                    act.wait_ge(ol_ready.sem, ol_ready.after(l, h + 1))
                    act.sem_inc(give_back(("PV", h)), 1)

                def take_heads(i):
                    a = full(l, ("YC", i))
                    act.copy(yc_t[:, i, :], a[:, 0:T]).then_inc(yc_ready.sem, 1)
                    act.wait_ge(yc_ready.sem, yc_ready.after(l, i + 1))
                    act.sem_inc(give_back(("YC", i)), 1)

                for h in range(HEADS):
                    for name in attention_order(h):
                        {"S": lambda: exps(*name[1:]), "T": lambda: take_turned(*name[1:]),
                         "PV": lambda: take_values(h), "YC": lambda: take_heads(h // 2)}[name[0]]()

                with act.Fori(0, D // CW) as i:
                    for n in range(6):
                        a = full(l, ("gate", n), i * 3)
                        act.wait_ge(merged_credit.sem, merged_credit.after(l, n + 1) + i * 6)
                        act.activation(gate_s[:, n % 2, 0:SAMPLE], a[:, 0:SAMPLE], ACT.Sigmoid)
                        act.activation(gate_s[:, n % 2, SAMPLE:T], a[:, 1024:1024 + P], ACT.Sigmoid)\
                            .then_inc(sig_ready.sem, 1)

                act.wait_ge(xmix_ready.sem, xmix_ready.after(l, KC))
                squares(l, KC)
                norm_root(l, "norm2", 1)
                add_shift(l, KC, 3 * KC)
                with act.Fori(0, 2) as i:
                    for n in range(8):
                        a = full(l, ("pq", n), i * 4)
                        act.copy(arena[:, bass.ds(i * (8 * T) + n * T, T)], a[:, 0:T]).then_inc(pq_ready.sem, 1)
                        act.wait_ge(pq_ready.sem, pq_ready.after(l, n + 1) + i * 8)
                        act.sem_inc(give_back(("pq", n)), 1)
                with act.Fori(0, TILES) as j:
                    act.wait_ge(soft_in.sem, soft_in.after(l, 1) + j)
                    act.activation(best_e, best_e, ACT.Exp).then_inc(soft_exp.sem, 1)
                act.wait_ge(sel_ready.sem, sel_ready.after(l, TILES))
                for j in range(TILES):
                    a = full(l, ("tok", j))
                    act.copy(tok_all[:, j, :], a[:, 0:D]).then_inc(tok_ready.sem, 1)
                    act.wait_ge(tok_ready.sem, tok_ready.after(l, j + 1))
                    act.sem_inc(give_back(("tok", j)), 1)

                with act.Fori(0, TILES) as j:
                    act.copy(tok_cur, m_flat[:, bass.ds(j * D, D)]).then_inc(tokc_ready.sem, 1)
                    for h in range(PH):
                        act.wait_ge(dots_ready.sem, dots_ready.after(l, h + 1) + j * PH)
                        act.activation(acts[:, h * TOPK:(h + 1) * TOPK], dots[:, h * TOPK:(h + 1) * TOPK],
                                       ACT.Gelu_apprx_tanh).then_inc(acts_ready.sem, 1)
                    a = full(l, ("peer", 0), j)
                    act.copy(y_tok, a[:, 0:D]).then_inc(ytok_ready.sem, 1)
                    act.wait_ge(ytok_ready.sem, ytok_ready.after(l, 1) + j)
                    act.sem_inc(give_back(("peer", 0)), 1)
                act.wait_ge(state_out.sem, state_out.after(l, 32))
                act.wait_ge(x_done.sem, x_done.after(l, TILES))

            last = FIRST_TURNS + LAYERS * TURNS
            squares(LAYERS, 0)
            act.wait_ge(acc_full[last % 2], last // 2 + 1)
            act.activation(root[:, :], accs[last % 2][:, 0:T], ACT.Sqrt, bias=eps_t[:, :]).then_inc(root_ready.sem, 1)
            act.wait_ge(root_ready.sem, root_ready.after(LAYERS, 1))
            act.sem_inc(acc_free[last % 2], 1)
            for j in range(TILES):
                g = last + 1 + j
                act.wait_ge(acc_full[g % 2], g // 2 + 1)
                act.copy(y_rows[:, j, :], accs[g % 2][:, 0:D]).then_inc(yrow_ready, 1)
                act.wait_ge(yrow_ready, j + 1)
                act.sem_inc(acc_free[g % 2], 1)

        @block.vector
        def _(dve):
            def full(l, name, more=0):
                dve.wait_ge(acc_full[TURN[name] % 2], turn_value(l, name, more))
                return acc(name)

            def give_back(name):
                dve.drain().then_inc(acc_free[TURN[name] % 2], 1)

            groups = ((0, slice(0, SAMPLE)), (1, slice(SAMPLE, T)))

            dve.wait_ge(x_in, 5 * 16)
            for g in range(TILES):
                dve.wait_ge(acc_full[g % 2], g // 2 + 1)
                dve.tensor_copy(x_t[:, :, g * P:(g + 1) * P],
                                accs[g % 2][:, 0:D].rearrange("p (k n) -> p k n", k=KC)).then_inc(x_ready, 1)
                dve.drain().then_inc(acc_free[g % 2], 1)
            dve.wait_ge(setup_done, 4)
            dve.wait_ge(cond_ready, 2)

            def normalise(l, first, which):
                dve.wait_ge(root_ready.sem, root_ready.after(l, first + 1))
                dve.reciprocal(rinv[:, :], root[:, :])
                dve.drain()
                for k in range(KC):
                    for g, cols in groups:
                        ins = dve.scalar_tensor_tensor(h_t[:, k, cols], x_t[:, k, cols], amp[:, which, k, g:g + 1],
                                                       rinv[:, cols], ALU.mult, ALU.mult)
                    ins.then_inc(scaled.sem, 1)

            with dve.Fori(0, LAYERS) as l:
                a = full(l, "params")
                dve.tensor_copy(par[:, :], a[:, 0:R_ALL]).then_inc(par_ready.sem, 1)
                give_back("params")
                a = full(l, "turned_a")
                dve.tensor_copy(turned[:, 0:6, :].rearrange("p a b -> p (a b)"), a[:, 0:6 * P])\
                    .then_inc(turned_ready.sem, 1)
                give_back("turned_a")
                a = full(l, "turned_b")
                dve.tensor_copy(turned[:, 6:10, :].rearrange("p a b -> p (a b)"), a[:, 0:4 * P])
                dve.tensor_copy(kt[:, :, T:T + PAST], a[:, 4 * P:6 * P].rearrange("p (a b) -> p a b", a=2))\
                    .then_inc(turned_ready.sem, 1)
                give_back("turned_b")
                a = full(l, "ada")
                dve.tensor_tensor(mod[:, :, :], a[:, 0:96].rearrange("p (n g) -> p n g", g=2),
                                  par[:, R_ADA:R_N1, None].to_broadcast([P, 6 * KC, 2]), ALU.add)
                give_back("ada")
                for n, row in ((0, R_N1), (1, R_N2)):
                    lo = (3 * n + 1) * KC
                    dve.scalar_tensor_tensor(amp[:, n], mod[:, lo:lo + KC, :], 1.0,
                                             par[:, row:row + KC, None].to_broadcast([P, KC, 2]), ALU.add, ALU.mult)
                dve.tensor_copy(g2_all[:, 0:STILES, :],
                                mod[:, None, 5 * KC:6 * KC, 0].to_broadcast([P, STILES, KC]))
                dve.tensor_copy(g2_all[:, STILES, :], mod[:, 5 * KC:6 * KC, 1])
                dve.drain().then_inc(mod_ready.sem, 1)
                normalise(l, 0, 0)

                dve.wait_ge(ssr_ready.sem, ssr_ready.after(l, 1))
                dve.wait_ge(zc_ready.sem, zc_ready.after(l, TILES))
                dve.reciprocal(sr[:, :, :], sr[:, :, :])
                dve.drain()
                kv = slice(Q_RANK, Q_RANK + KV_RANK)
                for j in range(TILES):
                    dve.tensor_scalar(zc[:, j, 0:Q_RANK], zc[:, j, 0:Q_RANK], sr[:, 0, j:j + 1], None, ALU.mult)
                    dve.scalar_tensor_tensor(zc[:, j, kv], zc[:, j, kv], sr[:, 1, j:j + 1], kvn[:, :],
                                             ALU.mult, ALU.mult)
                dve.drain().then_inc(lat_ready.sem, 1)

                for c in range(6):
                    a = full(l, ("conv", c))
                    w = [par[:, R_CW + tap * 6 + c:R_CW + tap * 6 + c + 1] for tap in range(3)]
                    dve.tensor_scalar(cv[:, c, :], a[:, 0:T], w[1], par[:, R_CB + c:R_CB + c + 1], ALU.mult, ALU.add)
                    dve.drain()
                    for _, cols in groups:
                        lo, hi = cols.start, cols.stop
                        dve.scalar_tensor_tensor(cv[:, c, lo + 1:hi], a[:, lo:hi - 1], w[0], cv[:, c, lo + 1:hi],
                                                 ALU.mult, ALU.add)
                    dve.drain()
                    for _, cols in groups:
                        lo, hi = cols.start, cols.stop
                        dve.scalar_tensor_tensor(cv[:, c, lo:hi - 1], a[:, lo + 1:hi], w[2], cv[:, c, lo:hi - 1],
                                                 ALU.mult, ALU.add)
                    give_back(("conv", c))
                dve.tensor_tensor(cv[:, 2:4, :], cv[:, 2:4, :], cv[:, 4:6, :], ALU.mult).then_inc(x1v_ready.sem, 1)
                a = full(l, "mix_a")
                dve.wait_ge(u_ready.sem, u_ready.after(l, 2))
                u_flat = u_t[:].rearrange("p k t -> p (k t)")
                for lo, hi in ((0, 512), (512, 1024), (1024, 2 * T)):
                    ins = dve.tensor_tensor(u_flat[:, lo:hi], u_flat[:, lo:hi], a[:, lo:hi], ALU.mult)
                ins.then_inc(ya_ready.sem, 1)
                give_back("mix_a")
                turns, magic = 0.15915494309189535, 12582912.0
                two_pi_hi, two_pi_lo, pi = 6.28125, 0.0019353071795864769, 3.1415925
                for n, (name, row) in enumerate((("filt1", R_B1), ("filt2", R_B2))):
                    a = full(l, name)
                    arg, k = hid[0:HID, n, :], root[0:HID, :]
                    dve.tensor_scalar(arg, a[0:HID, 0:T], par[0:HID, row:row + 1], None, ALU.add)
                    give_back(name)
                    dve.tensor_scalar(k, arg, turns, magic, ALU.mult, ALU.add)
                    dve.drain()
                    dve.tensor_scalar(k, k, magic, None, ALU.subtract)
                    dve.drain()
                    dve.scalar_tensor_tensor(arg, k, -two_pi_hi, arg, ALU.mult, ALU.add)
                    dve.drain()
                    dve.scalar_tensor_tensor(arg, k, -two_pi_lo, arg, ALU.mult, ALU.add)
                    dve.drain()
                    dve.tensor_scalar(arg, arg, pi, -pi, ALU.min, ALU.max).then_inc(arg_ready.sem, 1)
                dve.wait_ge(w_in_slot[CH_WIN % SLOTS].sem,
                            w_in_slot[CH_WIN % SLOTS].after(l, 16 * (CH_WIN // SLOTS + 1)))
                window = ring[:, CH_WIN % SLOTS, :].rearrange("p (j n) -> p j n", j=STILES)
                for name, tiles in (("filt3a", (0, 1, 2)), ("filt3b", (3, 4))):
                    a = full(l, name)
                    for n, j in enumerate(tiles):
                        w = window[:, j, :] if j < STILES else cst[:, C_WIN:C_WIN + 512]
                        dve.tensor_tensor(y_f[:, j, :], a[:, n * 512:(n + 1) * 512], w, ALU.mult)
                    give_back(name)
                dve.tensor_tensor(hy[:, :, 0:B_W], y_f[:, :, 0:B_W], y_f[:, :, B_W:], ALU.add)
                dve.tensor_tensor(hy[:, :, 2 * B_W:], y_f[:, :, 0:B_W], y_f[:, :, B_W:], ALU.subtract)
                dve.drain().then_inc(taps_ready.sem, 1)
                dve.wait_ge(spec_ready.sem, spec_ready.after(l, TILES))
                hc, uc, us, hs = (spec[:, :, n * B_W:(n + 1) * B_W] for n in range(4))
                for out, p, q, r, s, op in ((y_f[:, :, 0:B_W], uc, hc, us, hs, ALU.subtract),
                                            (y_f[:, :, B_W:], uc, hs, us, hc, ALU.add)):
                    dve.tensor_tensor(out, p, q, ALU.mult)
                    dve.tensor_tensor(tmp_f, r, s, ALU.mult)
                    dve.drain()
                    dve.tensor_tensor(out, out, tmp_f, op)
                    dve.drain()
                dve.drain().then_inc(yf_ready.sem, 1)
                for c in range(2):
                    a = full(l, ("idft", c))
                    dve.scalar_tensor_tensor(cv[:, 2 + c, :], cv[:, 2 + c, :], par[:, R_SK + c:R_SK + c + 1],
                                             a[:, 0:T], ALU.mult, ALU.add)
                    give_back(("idft", c))
                dve.tensor_tensor(cv[:, 2:4, :], cv[:, 2:4, :], cv[:, 0:2, :], ALU.mult).then_inc(yb_ready.sem, 1)

                for name, tiles in (("at_turn0", (0, 1, 2)), ("at_turn1", (3, 4))):
                    a = full(l, name)
                    for n, j in enumerate(tiles):
                        for c in range(2):
                            dve.tensor_scalar(zq_t[:, c, j * P:(j + 1) * P], a[:, n * 512 + c * P:n * 512 + (c + 1) * P],
                                              par[:, R_QN + c:R_QN + c + 1], None, ALU.mult)
                        dve.tensor_copy(kt[:, :, j * P:(j + 1) * P],
                                        a[:, n * 512 + 2 * P:n * 512 + 4 * P].rearrange("p (a b) -> p a b", a=2))
                    give_back(name)
                dve.drain().then_inc(lat_t_ready.sem, 1)
                a = full(l, "rope")
                cos, sin = cst[:, C_COS:C_COS + SAMPLE], cst[:, C_SIN:C_SIN + SAMPLE]
                dsts = (qp_t[:, 0, 0:SAMPLE], qp_t[:, 1, 0:SAMPLE], kt[:, 1, 0:SAMPLE])
                for n, dst in enumerate(dsts):
                    dve.tensor_tensor(rope_tmp[:, n, :], a[:, n * 512:(n + 1) * 512], sin, ALU.mult)
                    dve.tensor_tensor(dst, dst, cos, ALU.mult)
                give_back("rope")
                for n, dst in enumerate(dsts):
                    dve.tensor_tensor(dst, dst, rope_tmp[:, n, :], ALU.add)
                dve.drain().then_inc(rope_ready.sem, 1)

                def take_max(h, j):
                    m, width = h * TILES + j, T if j < STILES else P
                    a = full(l, ("S", h, j))
                    dve.tensor_reduce(stat[:, m % 2, 0:1], a[:, 0:width], AX.X, ALU.max)
                    dve.drain()
                    dve.tensor_scalar(stat[:, m % 2, 1:2], stat[:, m % 2, 0:1], -SCALE, None, ALU.mult)\
                        .then_inc(max_ready.sem, 1)

                def norm_probs(h, j):
                    m, width = h * TILES + j, T if j < STILES else P
                    dve.wait_ge(exp_ready.sem, exp_ready.after(l, m + 1))
                    dve.reciprocal(stat[:, m % 2, 3:4], stat[:, m % 2, 2:3])
                    dve.drain()
                    dve.tensor_scalar(prob[:, m % 2, 0:width], prob[:, m % 2, 0:width], stat[:, m % 2, 3:4], None,
                                      ALU.mult).then_inc(prob_ready.sem, 1)

                for h in range(HEADS):
                    for name in attention_order(h):
                        if name[0] == "S":
                            take_max(h, name[2])
                        elif name[0] == "T":
                            norm_probs(h, name[2])

                dve.drain().then_inc(merged_credit.sem, 2)
                with dve.Fori(0, D // CW) as i:
                    for n in range(6):
                        b, half = n // 2, n % 2
                        a = full(l, ("gate", n), i * 3)
                        dve.wait_ge(sig_ready.sem, sig_ready.after(l, n + 1) + i * 6)
                        out = m_flat[:, bass.ds((i * 2 + half) * T, T)]
                        dst = out if b == 0 else gate_y[:, half, :]
                        for lo, hi, at in ((0, SAMPLE, 512), (SAMPLE, T, 1024 + P)):
                            dve.tensor_tensor(dst[:, lo:hi], gate_s[:, half, lo:hi], a[:, at:at + hi - lo], ALU.mult)
                        give_back(("gate", n))
                        if b:
                            dve.tensor_tensor(out, out, gate_y[:, half, :], ALU.add)
                        dve.drain().then_inc(merged_ready.sem, 1)
                        dve.sem_inc(merged_credit.sem, 1)
                for n in range(KC):
                    a = full(l, ("out", n))
                    for g, cols in groups:
                        ins = dve.scalar_tensor_tensor(x_t[:, n, cols], a[:, cols], mod[:, 2 * KC + n, g:g + 1],
                                                       x_t[:, n, cols], ALU.mult, ALU.add)
                    ins.then_inc(xmix_ready.sem, 1)
                    give_back(("out", n))
                normalise(l, 1, 1)

                with dve.Fori(0, TILES) as j:
                    for n in range(2):
                        a = full(l, ("key", n), j)
                        carry_waits(dve, "dve")
                        hs = [(n * PH + g) for g in range(PH)]
                        src = [a[:, g * P:(g + 1) * P] for g in range(PH)]
                        rep = [repl[:, g * P:(g + 1) * P] for g in range(PH)]
                        for g, m in enumerate(hs):
                            dve.max(top_v[:, m // 2, m % 2, 0:8], src[g])
                        dve.drain()
                        for g, m in enumerate(hs):
                            dve.match_replace(rep[g], top_v[:, m // 2, m % 2, 0:8], src[g], -3.0e38)
                        dve.drain()
                        for g, m in enumerate(hs):
                            dve.max(top_v[:, m // 2, m % 2, 8:16], rep[g])
                        dve.drain()
                        for g, m in enumerate(hs):
                            for at in (0, 8):
                                dve.max_index(top_i[:, m // 2, m % 2, at:at + 8], top_v[:, m // 2, m % 2, at:at + 8],
                                              src[g] if at == 0 else rep[g])
                        give_back(("key", n))
                    dve.tensor_copy(top_f, top_i)
                    for h in range(PH):
                        dve.tensor_tensor(cand[:, h * 256:(h + 1) * 256].rearrange("p (a b) -> p a b", a=TOPK),
                                          top_v[:, h, 0, :, None].to_broadcast([P, TOPK, TOPK]),
                                          top_v[:, h, 1, None, :].to_broadcast([P, TOPK, TOPK]), ALU.add)
                    dve.drain()
                    src = [cand[:, h * 256:(h + 1) * 256] for h in range(PH)]
                    rep = [repl[:, h * 256:(h + 1) * 256] for h in range(PH)]
                    pos = best_p.rearrange("p (h k) -> p h k", h=PH)
                    for h in range(PH):
                        dve.max(best_v[:, h, 0:8], src[h])
                    dve.drain()
                    for h in range(PH):
                        dve.match_replace(rep[h], best_v[:, h, 0:8], src[h], -3.0e38)
                    dve.drain()
                    for h in range(PH):
                        dve.max(best_v[:, h, 8:16], rep[h])
                    dve.drain()
                    for h in range(PH):
                        for at in (0, 8):
                            dve.max_index(pos[:, h, at:at + 8], best_v[:, h, at:at + 8], src[h] if at == 0 else rep[h])
                    dve.tensor_tensor(best_e, best_v, best_v[:, :, 0:1].to_broadcast([P, PH, TOPK]), ALU.subtract)\
                        .then_inc(soft_in.sem, 1)
                    dve.drain()
                    dve.tensor_scalar(best_a[:, 0, :], best_p, 4, None, ALU.logical_shift_right)
                    dve.tensor_scalar(best_a[:, 1, :], best_p, 15, None, ALU.bitwise_and)
                    dve.drain()
                    dve.tensor_copy(best_f, best_a)
                    dve.drain()
                    for side in range(2):
                        hit = (cand if side == 0 else repl).rearrange("p (n k) -> p n k", k=TOPK)
                        dve.tensor_tensor(hit, best_f[:, side, :, None].to_broadcast([P, EXPERTS, TOPK]),
                                          cst[:, None, C_IOTA:C_IOTA + TOPK].to_broadcast([P, EXPERTS, TOPK]),
                                          ALU.is_equal)
                    dve.drain()
                    for side in range(2):
                        hit = (cand if side == 0 else repl).rearrange("p (h n k) -> p h n k", h=PH, k=TOPK)
                        dve.tensor_tensor(hit, hit, top_f[:, :, side, None, :].to_broadcast([P, PH, TOPK, TOPK]),
                                          ALU.mult)
                    dve.drain()
                    for side in range(2):
                        hit = (cand if side == 0 else repl).rearrange("p (n k) -> p n k", k=TOPK)
                        dve.tensor_reduce(best_i[:, side, :], hit, AX.X, ALU.add)
                    dve.drain()
                    dve.scalar_tensor_tensor(best_i[:, 0, :], best_i[:, 0, :], float(NKEYS), best_i[:, 1, :],
                                             ALU.mult, ALU.add)
                    dve.drain()
                    dve.tensor_scalar(idx_flat[:, bass.ds(j * EXPERTS, EXPERTS)], best_i[:, 0, :], table_base[:, :],
                                      None, ALU.add)
                    dve.wait_ge(soft_exp.sem, soft_exp.after(l, 1) + j)
                    dve.tensor_reduce(best_s, best_e, AX.X, ALU.add)
                    dve.drain()
                    dve.reciprocal(best_r, best_s)
                    dve.drain()
                    dve.tensor_tensor(g_flat[:, bass.ds(j * EXPERTS, EXPERTS)].rearrange("p (h k) -> p h k", h=PH),
                                      best_e, best_r[:, :, None].to_broadcast([P, PH, TOPK]), ALU.mult)
                    dve.drain().then_inc(sel_ready.sem, 1)

                dve.tensor_scalar(table_base[:, :], table_base[:, :], float(NKEYS * NKEYS), None, ALU.add)

                with dve.Fori(0, TILES) as j:
                    dve.tensor_copy(g_cur[:, :], g_flat[:, bass.ds(j * EXPERTS, EXPERTS)])
                    dve.tensor_copy(g2_cur[:, :], g2_all[:].rearrange("p j k -> p (j k)")[:, bass.ds(j * KC, KC)])
                    dve.drain()
                    dve.wait_ge(tokc_ready.sem, tokc_ready.after(l, 1) + j)
                    for h in range(PH + 1):
                        if h:
                            if h >= 3:
                                dve.wait_ge(rows_v_free.sem,
                                            rows_v_free.after(l, (h - 2) * TOPK) + j * EXPERTS)
                            dve.wait_ge(acts_ready.sem, acts_ready.after(l, h) + j * PH)
                            for k in range(TOPK):
                                n = (h - 1) * TOPK + k
                                ins = dve.tensor_scalar(diag[(h - 1) % 2][:, k, :], ident, acts[:, n:n + 1],
                                                        g_cur[:, n:n + 1], ALU.mult, ALU.mult)
                            ins.then_inc(diag_ready.sem, 1)
                        if h < PH:
                            for k in range(TOPK):
                                n = h * TOPK + k
                                s = n % ROWS_U
                                dve.wait_ge(rows_u_in[s].sem,
                                            rows_u_in[s].after(l, 16 * (n // ROWS_U + 1)) + j * (16 * EXPERTS // ROWS_U))
                                dve.tensor_tensor_reduce(rows_u[:, s, :], rows_u[:, s, :], tok_cur, 1.0, 0.0, ALU.mult,
                                                         ALU.add, dots[:, n:n + 1]).then_inc(rows_u_free.sem, 1)
                            dve.drain().then_inc(dots_ready.sem, 1)
                    a = full(l, ("peer", 1), j)
                    for k in range(KC):
                        at = x_t[:, k, bass.ds(j * P, P)]
                        dve.scalar_tensor_tensor(at, a[:, k * P:(k + 1) * P], g2_cur[:, k:k + 1], at,
                                                 ALU.mult, ALU.add)
                    give_back(("peer", 1))
                    dve.drain().then_inc(x_done.sem, 1)

            dve.wait_ge(root_ready.sem, root_ready.after(LAYERS, 1))
            dve.reciprocal(rinv[:, :], root[:, :])
            dve.drain()
            for k in range(KC):
                dve.scalar_tensor_tensor(h_t[:, k, :], x_t[:, k, :], cond_t[:, 2, k:k + 1], rinv[:, :],
                                         ALU.mult, ALU.mult)
            dve.drain().then_inc(fin_ready, 1)

        @block.gpsimd
        def _(pool):
            pool.memset(par_rows[:, :], 0.0).then_inc(par_zero, 1)
            pool.memset(mean_w[:, :], 1.0 / D).then_inc(setup_done, 1)
            pool.memset(one_row[:, :], 1.0).then_inc(setup_done, 1)
            pool.memset(eps_t[:, :], EPS).then_inc(setup_done, 1)
            pool.memset(table_base[:, :], 0.0).then_inc(setup_done, 1)
            pool.sem_inc(rows_u_free.sem, ROWS_U)
            pool.sem_inc(rows_v_free.sem, ROWS_V)

            def gather(rows, idx, free, came, table, l, j, n, slots):
                s = n % slots
                pool.wait_ge(free.sem, free.after(l, n + 1 - slots) + j * EXPERTS)
                carry_waits(pool, "pool")
                pool.indirect_dma_start(rows[:, s, :], None, table, bass.IndirectOffsetOnAxis(
                    ap=idx[:, n:n + 1], axis=0)).then_inc(came[s].sem, 16)

            u_rows, v_rows = (w.rearrange("l n d -> (l n) d") for w in (peer_u, peer_v))
            with pool.Fori(0, LAYERS) as l:
                pool.wait_ge(tok_ready.sem, tok_ready.after(l, TILES))
                carry_waits(pool, "pool")
                with pool.Fori(0, TILES) as j:
                    here = idx_flat[:, bass.ds(j * EXPERTS, EXPERTS)]
                    pool.tensor_copy(idx_u, here)
                    pool.drain()
                    for h in range(PH + 1):
                        if h == 1:
                            pool.wait_ge(rows_v_free.sem, rows_v_free.after(l, 0) + j * EXPERTS)
                            carry_waits(pool, "pool")
                            pool.tensor_copy(idx_v, here)
                            pool.drain()
                        for k in range(TOPK):
                            if h < PH:
                                gather(rows_u, idx_u, rows_u_free, rows_u_in, u_rows, l, j, h * TOPK + k, ROWS_U)
                            if h:
                                gather(rows_v, idx_v, rows_v_free, rows_v_in, v_rows, l, j, (h - 1) * TOPK + k, ROWS_V)
                    for s in range(ROWS_U):
                        pool.wait_ge(rows_u_in[s].sem, rows_u_in[s].after(l, 16 * EXPERTS // ROWS_U)
                                     + j * (16 * EXPERTS // ROWS_U))
                    carry_waits(pool, "pool")


_INS = ['x_prompt', 'x_sample', 'cache_ckv', 'cache_kpe', 'c', 'c_ctx', 'w_ada', 'b_ada', 'norm1', 'norm2', 'w_in',
        'a_ws', 'a_bs', 'b_conv_w', 'b_conv_b', 'b_filt_w1', 'b_filt_b1', 'b_filt_w2', 'b_filt_b2', 'b_filt_w3',
        'b_skip', 'q_norm', 'kv_norm', 'w_uq', 'w_uk', 'w_uv', 'w_branch_a', 'w_branch_b', 'w_branch_c', 'w_out',
        'peer_wq', 'peer_sub_keys', 'peer_u', 'peer_v', 'final_norm']
_OUTS = [((1, PROMPT, D), 'float32'), ((1, SAMPLE, D), 'float32'), ((1, LAYERS, PROMPT, KV_RANK), 'float32'),
         ((1, LAYERS, PROMPT, ROPE), 'float32')]


def shape_constants():
    import math

    import numpy as np

    f32 = np.float32

    def transform(length):
        theta = math.pi * np.outer(np.arange(length), np.arange(length) + 0.5) / length
        return np.cos(theta), np.sin(theta), np.cos(theta).T / length, np.sin(theta).T / length

    def positions(length):
        t = np.linspace(0.0, 1.0, length, dtype=f32)[:, None]
        bands = (EMB - 1) // 2
        f = np.linspace(1e-4, bands - 1, bands, dtype=f32)
        w = (f32(2.0 * math.pi) * np.arange(length, dtype=f32)[:, None] / f32(length)).astype(f32)
        z = np.concatenate([t, np.cos(f * w), -np.sin(f * w)], axis=-1)
        deltas = np.abs(np.linspace(math.log(1e-2) / 0.3, math.log(1e-2) / 1.5, B_W, dtype=f32))
        fwd = np.exp(-t * deltas)
        bwd = fwd.copy()
        bwd[0] = 0.0
        return z.T, np.concatenate([fwd, bwd], axis=1)

    def by_partition(m):
        return m.reshape(STILES, P, -1).transpose(1, 0, 2).reshape(P, -1)

    cst = np.zeros((P, C_ALL), f32)
    cst[:, C_ID:C_ID + P] = np.eye(P)
    cst[:, C_DFT:C_DFT + 4 * P] = np.concatenate(transform(PROMPT), axis=1)
    tok = np.arange(SAMPLE)
    quarter = ROPE // 4
    inv = (f32(10000.0) ** (-np.arange(quarter, dtype=f32) / quarter)).astype(f32)
    for r in range(P):
        axis, half, f = r % ROPE // (2 * quarter), r % (2 * quarter) // quarter, r % quarter
        ang = (tok // 64 if axis == 0 else tok % 64).astype(f32) * inv[f]
        cst[r, C_COS:C_COS + SAMPLE] = np.cos(ang)
        cst[r, C_SIN:C_SIN + SAMPLE] = np.sin(ang)
        other = r + quarter if half == 0 else r - quarter
        cst[other, C_PERM + r] = -1.0 if half == 0 else 1.0
    z_s, win_s = positions(SAMPLE)
    z_p, win_p = positions(PROMPT)
    cst[:, C_WIN:C_WIN + 512] = win_p
    cst[0:EMB, C_Z:C_Z + SAMPLE] = z_s
    cst[0:EMB, C_Z + SAMPLE:C_Z + T] = z_p
    cst[:, C_IOTA:C_IOTA + 16] = np.arange(16)
    tables = np.stack([by_partition(m) for m in (win_s, *transform(SAMPLE))]).astype(f32)
    return cst, tables


def kernel(**inputs):
    import numpy as _np
    import concourse.bacc as _bacc
    from concourse import mybir as _mybir
    from concourse.bass_utils import run_bass_kernel_spmd as _run

    nc = _bacc.Bacc("TRN2", target_bir_lowering=False, num_devices=1)
    cst, tables = shape_constants()
    arrays, args = {}, []
    for name, a in [(n, inputs[n]) for n in _INS] + [("consts", cst), ("tables", tables)]:
        a = _np.ascontiguousarray(a)
        arrays[f"in_{name}_dram"] = a
        args.append(nc.dram_tensor(f"in_{name}_dram", a.shape, _mybir.dt.from_np(a.dtype), kind="ExternalInput").ap())
    for i, (shape, dtype) in enumerate(_OUTS):
        dt = _mybir.dt.from_np(_np.dtype(dtype))
        args.append(nc.dram_tensor(f"out_{i}_dram", shape, dt, kind="ExternalOutput").ap())
    build(nc, *args)
    r = _run(nc, [arrays], core_ids=[0])
    return tuple(r.results[0][f"out_{i}_dram"] for i in range(len(_OUTS)))
```

```python
from contextlib import ExitStack

import concourse.bass as bass
from concourse import mybir

ALU = mybir.AluOpType
ACT = mybir.ActivationFunctionType
AX = mybir.AxisListType
F32 = mybir.dt.float32
U32 = mybir.dt.uint32

P = 128
D = 1024
KC = D // P
LAYERS = 2
SAMPLE, PROMPT, PAST = 512, 128, 128
T = SAMPLE + PROMPT
TILES = T // P
STILES = SAMPLE // P
EPS = 1e-6
A_W = B_W = 256
HEADS, NOPE, ROPE, VD = 8, 64, 32, 64
Q_RANK, KV_RANK = 256, 128
QH = NOPE + ROPE
SCALE = float(QH) ** -0.5
EMB, HID = 33, 64
PH, TOPK, NKEYS = 8, 16, 128
EXPERTS = PH * TOPK

COL_U = 3 * D
COL_V = COL_U + A_W
COL_B = COL_V + A_W
COL_Q = COL_B + 3 * B_W
COL_KV = COL_Q + Q_RANK
KV_COLS = KV_RANK + ROPE

SLOTS = 4
CW = 256
N_ADA = 6 * D // CW
CH_Q = N_ADA
CH_B = CH_Q + 4
CH_WIN = CH_B + 3
CH_DFT = CH_WIN + 1
CH_GATE = CH_DFT + 4
CH_OUT = CH_GATE + 4 * (D // CW)
CH_PQ = CH_OUT + D // CW
CHUNKS = CH_PQ + PH * 2 * P // CW
assert CHUNKS % SLOTS == 0 and CH_GATE % SLOTS == 0 and CH_PQ % SLOTS == 0

R_ADA, R_N1, R_N2, R_CW, R_CB, R_SK, R_QN, R_B1, R_B2 = 0, 48, 56, 64, 82, 88, 90, 92, 93
R_ALL = 94

C_ID, C_DFT, C_COS, C_SIN, C_PERM, C_WIN, C_Z = 0, 128, 640, 1152, 1664, 1792, 2304
C_IOTA = C_Z + T
C_Q = C_IOTA + 16
C_ALL = C_Q + T

ROWS_U, ROWS_V = 4, 4
LAST = EXPERTS - TOPK
H_TOK = 4


def turn_table():
    order = [("ada", n) for n in range(N_ADA)] + ["params", "turned", "filt1", "mod", "norm1", "filt2"]
    order += [("token", j) for j in range(TILES)] + [("u", c) for c in range(2)] + [("conv", c) for c in range(2)]
    order += ["filt3a", "filt3b"] + [("conv", c) for c in range(2, 6)] + ["mix_a", "hy_turn", "at_turn0", "at_turn1"]
    order += [("dft", j) for j in range(TILES)] + [("idft", c) for c in range(2)]
    order += ["rope"] + [("q", h) for h in range(HEADS)]
    order += [("S", m) for m in range(HEADS * TILES)]
    order += [("gate", n) for n in range(3 * KC)] + [("out", n) for n in range(KC)] + ["norm2"]
    order += [("pq", n) for n in range(2 * PH)] + [("key", 0), ("key", 1), "tok"]
    for j in range(TILES - 1):
        names = [("next_key", 0), ("next_key", 1), "next_tok", "peer_out"]
        order += names if j == 0 else [(name, j) for name in names]
    order += ["peer_last"]
    assert len(order) % 2 == 0, len(order)
    return {name: n for n, name in enumerate(order)}


PAIRS = HEADS * TILES
VALUES_LAG = TILES + 2
STEPS = PAIRS + VALUES_LAG + 2


def side_turns(m):
    turns = []
    if 2 <= m < PAIRS + 2:
        turns.append(("T", m - 2))
    if m % TILES == 1 and m // TILES + 1 < HEADS:
        turns.append(("K", m // TILES + 1))
    last = m - 2 - VALUES_LAG + 1
    if last > 0 and last % (2 * TILES) == 0:
        turns.append(("Y", last // (2 * TILES) - 1))
    return turns


def side_table():
    order = [("K", 0)] + [name for m in range(STEPS) for name in side_turns(m)]
    return {name: n for n, name in enumerate(order)}


SIDE = side_table()
assert len(SIDE) == PAIRS + HEADS + HEADS // 2


TURN = turn_table()
TURNS = len(TURN)
FIRST_TURNS = TILES + 1


def turn_value(l, name, more=0):
    return FIRST_TURNS // 2 + l * (TURNS // 2) + TURN[name] // 2 + 1 + more


class Signal:

    def __init__(self, sem, layer, first=0):
        self.sem, self.layer, self.first = sem, layer, first

    def after(self, l, n):
        return self.first + l * self.layer + n


def build(nc, x_prompt, x_sample, cache_ckv, cache_kpe, c, c_ctx, w_ada, b_ada, norm1, norm2, w_in,
          a_ws, a_bs, b_conv_w, b_conv_b, b_filt_w1, b_filt_b1, b_filt_w2, b_filt_b2, b_filt_w3, b_skip,
          q_norm, kv_norm, w_uq, w_uk, w_uv, w_branch_a, w_branch_b, w_branch_c, w_out,
          peer_wq, peer_sub_keys, peer_u, peer_v, final_norm, consts, tables,
          y_prompt, y_sample, state_ckv, state_kpe):
    with ExitStack() as ctx:
        def sb(name, shape, dt=F32):
            return ctx.enter_context(nc.sbuf_tensor(name, shape, dt))

        def sem(name):
            return ctx.enter_context(nc.semaphore(name))

        def signal(name, layer, first=0):
            return Signal(sem(name), layer, first)

        cst = sb("cst", [P, C_ALL])
        ident = cst[:, C_ID:C_ID + P]
        x_t = sb("x_t", [P, KC, T])
        h_t = sb("h_t", [P, KC, T])
        m_t = sb("m_t", [P, KC, T])
        ring = sb("ring", [P, SLOTS, KC * CW])
        mean_w = sb("mean_w", [P, P])
        one_row = sb("one_row", [1, NOPE])
        eps_t = sb("eps_t", [P, 1])
        cond_rows = sb("cond_rows", [3 * KC, P])
        cond_t = sb("cond_t", [P, 3, KC])
        par_rows = sb("par_rows", [R_ALL, P])
        par = sb("par", [P, R_ALL])
        kvn = sb("kvn", [P, KV_RANK])
        abs_row = sb("abs_row", [1, 4, P])
        past = sb("past", [P, 2, P])
        uv = sb("uv", [P, HEADS * VD])
        uq = sb("uq", [P, 2, HEADS, P])
        uk = sb("uk", [P, HEADS * NOPE])
        f_w1 = sb("f_w1", [EMB, HID])
        f_w2 = sb("f_w2", [HID, HID])
        turned = sb("turned", [P, 6, P])
        mod = sb("mod", [P, 6 * KC, 2])
        amp = sb("amp", [P, 2, KC, 2])
        root = sb("root", [P, T])
        rinv = root
        u_t = sb("u_t", [P, 2, T])
        cv = sb("cv", [P, 6, T])
        zc = sb("zc", [P, TILES, 512])
        ss = sb("ss", [P, 2, TILES])
        sr = sb("sr", [P, 2, TILES])
        kt = sb("kt", [P, 2, T + PAST])
        stat = sb("stat", [P, 4, 3])
        g2_all = sb("g2_all", [P, TILES, KC])
        g2_cur = sb("g2_cur", [P, KC])
        table_base = sb("table_base", [P, 1])
        ARENA = 2 * PH * T
        arena = sb("arena", [P, ARENA])

        def view(start, *dims):
            n = 1
            for d in dims:
                n *= d
            assert start + n <= ARENA
            flat = arena[:, start:start + n]
            if len(dims) == 1:
                return flat
            names = " ".join("abc"[:len(dims)])
            return flat.rearrange(f"p ({names}) -> p {names}", **dict(zip("abc", dims)))

        ws_in = view(0, 6, P)
        mod_rows = view(6 * P, 6 * D)
        f_w3 = view(7040, 2 * B_W)[0:HID, :]
        dump = view(0, TILES, Q_RANK + KV_RANK)
        hy = view(0, TILES, 3 * B_W)
        y_f = view(3840, TILES, 2 * B_W)
        tmp_f = view(6400, 2, B_W)
        hid = view(7680, 2, T)
        v_tok = view(8960, TILES, A_W)
        spec = m_t[:].rearrange("p k t -> p (k t)").rearrange("p (j n) -> p j n", j=TILES)
        prob = view(0, 3, T)
        prob_t = [view(3 * T + n * 2560, TILES, SAMPLE) for n in range(2)]
        k_h = [view(3 * T + 5120 + n * (T + PAST), T + PAST) for n in range(2)]
        prob_tp = [view(3 * T + 5120 + (2 * T + 2 * PAST) + n * P, P) for n in range(2)]
        zq_t = view(8960, 2, T)
        ol_t = zq_t
        rope_tmp = view(0, SAMPLE)
        q_t = m_t
        yc_k = [cv[:, k, :] for k in (0, 1, 4, 5)]
        gate_s = view(0, 2, T)
        gate_y = view(2 * T, 2, T)
        pq_t = view(0, 2 * PH, T)
        m_flat = m_t[:].rearrange("p k t -> p (k t)")
        cv_flat = cv[:].rearrange("p k t -> p (k t)")
        u_flat = u_t[:].rearrange("p k t -> p (k t)")
        cand = cv_flat[:, 0:2048]
        repl = u_flat[:, 0:1024]
        zc_flat = zc[:].rearrange("p j n -> p (j n)")
        top_v = zc_flat[:, 0:256].rearrange("p (h s k) -> p h s k", h=PH, s=2)
        top_i = zc_flat[:, 256:512].bitcast(U32).rearrange("p (h s k) -> p h s k", h=PH, s=2)
        top_f = zc_flat[:, 512:768].rearrange("p (h s k) -> p h s k", h=PH, s=2)
        best_v = zc_flat[:, 768:896].rearrange("p (h k) -> p h k", h=PH)
        best_p = zc_flat[:, 896:1024].bitcast(U32)
        best_a = zc_flat[:, 1024:1280].bitcast(U32).rearrange("p (s n) -> p s n", s=2)
        best_f = zc_flat[:, 1280:1536].rearrange("p (s n) -> p s n", s=2)
        best_i = zc_flat[:, 1536:1792].rearrange("p (s n) -> p s n", s=2)
        best_e = zc_flat[:, 1792:1920].rearrange("p (h k) -> p h k", h=PH)
        best_s = zc_flat[:, 1920:1928]
        best_r = zc_flat[:, 1928:1936]
        kt_flat = kt[:].rearrange("p a n -> p (a n)")
        idx_u, idx_v = kt_flat[:, 0:P].bitcast(U32), kt_flat[:, 4 * P:5 * P].bitcast(U32)
        g_cur = kt_flat[:, P:2 * P]
        dots, acts = kt_flat[:, 2 * P:3 * P], kt_flat[:, 3 * P:4 * P]
        idx_last = idx_v[:, 0:TOPK]
        idx_next, g_next = kt_flat[:, 5 * P:6 * P].bitcast(U32), kt_flat[:, 6 * P:7 * P]
        ring_flat = ring[:].rearrange("p s n -> p (s n)")
        rows_u = ring_flat[:, 0:ROWS_U * D].rearrange("p (s n) -> p s n", s=ROWS_U)
        rows_v = ring_flat[:, ROWS_U * D:(ROWS_U + ROWS_V) * D].rearrange("p (s n) -> p s n", s=ROWS_V)
        diag = [m_flat[:, n * TOPK * P:(n + 1) * TOPK * P].rearrange("p (k n) -> p k n", k=TOPK) for n in range(2)]
        tok_cur = m_flat[:, 4096:4096 + D]
        stage = cv_flat[:, 2048:2048 + D].rearrange("p (k n) -> p k n", k=KC)
        y_tok = uq[:].rearrange("p k h n -> p (k h n)")[:, 0:D]
        x_rows = view(0, TILES, D)
        y_rows = view(0, TILES, D)

        ps = ctx.enter_context(nc.psum_tensor("ps", [P, 8 * 512], F32))
        accs = [ps[:, 0:1536], ps[:, 1536:3072]]
        y_acc = ps[:, 3072:4096]
        side = y_acc
        values_at = ((0, SAMPLE, ps[:, 1024:1536]), (SAMPLE, T, ps[:, 2560:2560 + P]))

        def acc(name):
            return accs[TURN[name] % 2]

        acc_full = [sem("acc_full0"), sem("acc_full1")]
        acc_free = [sem("acc_free0"), sem("acc_free1")]
        consts_in, x_in = sem("consts_in"), sem("x_in")
        setup_done = sem("setup_done")
        par_zero = sem("par_zero")
        x_ready = sem("x_ready")
        cond_ready = sem("cond_ready")
        PARAM_DMAS = 25
        params_in = signal("params_in", 16 * PARAM_DMAS)
        w_in_slot = [signal(f"w_slot{s}", 16 * (CHUNKS // SLOTS - (D // CW if s == SLOTS - 1 else 0)))
                     for s in range(SLOTS)]
        branch_in = signal("branch_in", 16 * 3 * (D // CW))
        w_free = signal("w_free", CHUNKS, SLOTS)
        par_ready = signal("par_ready", 1)
        turned_ready = signal("turned_ready", 1)
        mod_ready = signal("mod_ready", 1)
        sq_ready = signal("sq_ready", 2 * KC)
        root_ready = signal("root_ready", 2)
        scaled = signal("scaled", 2 * KC)
        h_ready = signal("h_ready", 2 * KC)
        zc_ready = signal("zc_ready", TILES)
        u_ready = signal("u_ready", 2)
        ya_ready = signal("ya_ready", 1)
        x1v_ready = signal("x1v_ready", 1)
        hyu_ready = signal("hyu_ready", 1)
        arg_ready = signal("arg_ready", 2)
        sin_ready = signal("sin_ready", 2)
        taps_ready = signal("taps_ready", 1)
        spec_ready = signal("spec_ready", TILES)
        yf_ready = signal("yf_ready", 1)
        yb_ready = signal("yb_ready", 1)
        ssr_ready = signal("ssr_ready", 1)
        lat_ready = signal("lat_ready", 1)
        state_out = signal("state_out", 32)
        lat_t_ready = signal("lat_t_ready", 1)
        uq_ready = signal("uq_ready", 1)
        adac_ready = signal("adac_ready", N_ADA)
        q_ready = signal("q_ready", HEADS)
        rope_ready = signal("rope_ready", 1)
        k_ready = signal("k_ready", HEADS)
        side_full = signal("side_full", len(SIDE))
        side_free = signal("side_free", len(SIDE), 1)
        max_ready = signal("max_ready", PAIRS)
        exp_ready = signal("exp_ready", PAIRS)
        prob_ready = signal("prob_ready", PAIRS)
        values_full = signal("values_full", HEADS)
        ol_ready = signal("ol_ready", HEADS)
        yc_ready = signal("yc_ready", HEADS // 2)
        sig_ready = signal("sig_ready", 3 * KC)
        merged_credit = signal("merged_credit", 3 * KC + 2)
        merged_ready = signal("merged_ready", 3 * KC)
        xmix_ready = signal("xmix_ready", KC)
        pq_ready = signal("pq_ready", 2 * PH)
        soft_in = signal("soft_in", TILES)
        soft_exp = signal("soft_exp", TILES)
        idx_ready = signal("idx_ready", TILES)
        last_ready = signal("last_ready", TILES)
        tok_ready = signal("tok_ready", TILES)
        stage_ready = signal("stage_ready", 3 * (TILES - 1))
        y_full = signal("y_full", TILES)
        rows_u_in = [signal(f"rows_u_in{s}", 16 * TILES * EXPERTS // ROWS_U) for s in range(ROWS_U)]
        rows_v_in = [signal(f"rows_v_in{s}", 16 * TILES * EXPERTS // ROWS_V) for s in range(ROWS_V)]
        rows_u_free = signal("rows_u_free", TILES * EXPERTS, ROWS_U)
        rows_v_free = signal("rows_v_free", TILES * EXPERTS, ROWS_V)
        dots_ready = signal("dots_ready", TILES * PH)
        acts_ready = signal("acts_ready", TILES * PH)
        diag_ready = signal("diag_ready", TILES * PH)
        ytok_ready = signal("ytok_ready", TILES)
        x_done = signal("x_done", TILES)
        fin_ready = sem("fin_ready")
        yrow_ready = sem("yrow_ready")
        y_out = sem("y_out")

        passed = {"pe": sem("passed_pe"), "dve": sem("passed_dve"), "pool": sem("passed_pool"),
                  "sp": sem("passed_sp")}

        def carry_waits(eng, name):
            eng.sem_inc(passed[name], 1)

        block = ctx.enter_context(nc.Block())

        @block.sync
        def _(sp):
            sp.dma_start(cst[:], consts).then_inc(consts_in, 16)
            sp.dma_start(cond_rows[0:KC, :], c.rearrange("a (k p) -> (a k) p", p=P)).then_inc(x_in, 16)
            sp.dma_start(cond_rows[KC:2 * KC, :], c_ctx.rearrange("(k p) -> k p", p=P)).then_inc(x_in, 16)
            sp.dma_start(cond_rows[2 * KC:, :], final_norm.rearrange("(k p) -> k p", p=P)).then_inc(x_in, 16)
            sp.dma_start(x_rows[:, 0:STILES, :], x_sample[0].rearrange("(j p) d -> p j d", p=P)).then_inc(x_in, 16)
            sp.dma_start(x_rows[:, STILES, :], x_prompt[0]).then_inc(x_in, 16)

            def load(l, n, src, more=0):
                slot = n % SLOTS
                k, cols = src.shape[1], src.shape[2]
                sp.wait_ge(w_free.sem, l * CHUNKS + n + more + 1)
                sp.dma_start(ring[:, slot, 0:k * cols].rearrange("p (k n) -> p k n", k=k), src)\
                    .then_inc(w_in_slot[slot].sem, 16)

            def cols_of(w, l, start, n=CW):
                return w[l, :, bass.ds(start, n)].rearrange("(k p) n -> p k n", p=P)

            with sp.Fori(0, LAYERS) as l:
                with sp.Fori(0, N_ADA // SLOTS) as i:
                    for s in range(SLOTS):
                        load(l, s, cols_of(w_ada, l, (i * SLOTS + s) * CW), i * SLOTS)
                load(l, CH_Q, cols_of(w_in, l, COL_Q))
                load(l, CH_Q + 1, cols_of(w_in, l, COL_KV, KV_COLS))
                load(l, CH_Q + 2, cols_of(w_in, l, COL_V))
                load(l, CH_Q + 3, cols_of(w_in, l, COL_U))
                for s in range(3):
                    load(l, CH_B + s, cols_of(w_in, l, COL_B + s * CW))
                for s in range(5):
                    load(l, CH_WIN + s, tables[s].rearrange("p (j n) -> p j n", j=STILES))
                with sp.Fori(0, D // CW) as i:
                    for s in range(3):
                        load(l, CH_GATE + s, cols_of(w_in, l, s * D + i * CW), i * SLOTS)
                    sp.wait_ge(w_free.sem, l * CHUNKS + CH_GATE + 3 + i * SLOTS + 1)
                    stack = ring[:, 3, :].rearrange("p (k n) -> p k n", k=KC)
                    k0 = 0
                    for w in (w_branch_a, w_branch_b, w_branch_c):
                        k = w.shape[1] // P
                        sp.dma_start(stack[:, k0:k0 + k, :], cols_of(w, l, i * CW)).then_inc(branch_in.sem, 16)
                        k0 += k
                for s in range(D // CW):
                    load(l, CH_OUT + s, cols_of(w_out, l, s * CW))
                with sp.Fori(0, 2) as i:
                    for s in range(SLOTS):
                        load(l, CH_PQ + s, cols_of(peer_wq, l, (i * SLOTS + s) * CW), i * SLOTS)
                sp.wait_ge(x_done.sem, x_done.after(l, TILES))
                carry_waits(sp, "sp")
            for j in range(TILES):
                sp.wait_ge(yrow_ready, j + 1)
                dst = y_sample[0, j * P:(j + 1) * P, :] if j < STILES else y_prompt[0]
                sp.dma_start(dst, y_rows[:, j, :]).then_inc(y_out, 16)
            sp.wait_ge(y_out, 16 * TILES)

        @block.tensor
        def _(pe):
            def open_turn(l, name, more=0):
                pe.wait_ge(acc_free[TURN[name] % 2], turn_value(l, name, more))
                return acc(name)

            def close_turn(name, mm):
                mm.then_inc(acc_full[TURN[name] % 2], 1)

            def release(n):
                pe.drain().then_inc(w_free.sem, n)

            def chunk_arrived(l, n, more=0):
                slot, m = n % SLOTS, n // SLOTS + 1
                if slot == SLOTS - 1 and n >= CH_OUT:
                    m -= D // CW
                pe.wait_ge(w_in_slot[slot].sem, w_in_slot[slot].after(l, 16 * m) + 16 * more)
                return ring[:, slot, :].rearrange("p (k n) -> p k n", k=KC)

            def product(a, lhs, rhs, arriving=None):
                n = len(lhs)
                for lo, hi in ((0, SAMPLE), (SAMPLE, T)):
                    for k in range(n):
                        if arriving is not None and lo == 0:
                            pe.wait_ge(h_ready.sem, arriving + (k + 1))
                        mm = pe.matmul(a[:, lo:hi], lhs[k], rhs[k][:, lo:hi], start=k == 0, stop=k == n - 1)
                return mm

            def blocks(w, c0):
                return [w[:, k, c0:c0 + P] for k in range(KC)]

            h_k = [h_t[:, k, :] for k in range(KC)]

            pe.sem_inc(acc_free[0], 1)
            pe.sem_inc(acc_free[1], 1)
            pe.sem_inc(side_free.sem, 1)
            pe.sem_inc(w_free.sem, SLOTS)
            pe.wait_ge(consts_in, 16)
            pe.wait_ge(x_in, 5 * 16)
            for g in range(TILES):
                pe.wait_ge(acc_free[g % 2], g // 2 + 1)
                for k in range(KC):
                    mm = pe.transpose(accs[g % 2][:, k * P:(k + 1) * P], x_rows[:, g, k * P:(k + 1) * P], ident)
                mm.then_inc(acc_full[g % 2], 1)
            pe.wait_ge(acc_free[TILES % 2], TILES // 2 + 1)
            pe.transpose(accs[TILES % 2][:, 0:3 * KC], cond_rows[:, :], ident[0:3 * KC, 0:3 * KC])\
                .then_inc(acc_full[TILES % 2], 1)

            def root_mean(l, name, first):
                a = open_turn(l, name)
                for lo, hi in ((0, SAMPLE), (SAMPLE, T)):
                    for k in range(KC):
                        if lo == 0:
                            pe.wait_ge(sq_ready.sem, sq_ready.after(l, first + k + 1))
                        mm = pe.matmul(a[:, lo:hi], mean_w[:], m_t[:, k, lo:hi], start=k == 0, stop=k == KC - 1)
                close_turn(name, mm)

            with pe.Fori(0, LAYERS) as l:
                pe.wait_ge(cond_ready, 2)
                carry_waits(pe, "pe")
                with pe.Fori(0, N_ADA // SLOTS) as i:
                    for s in range(SLOTS):
                        w = chunk_arrived(l, s, i)
                        a = open_turn(l, ("ada", s), i * 2)
                        for k in range(KC):
                            mm = pe.matmul(a[0:2, 0:CW], cond_t[:, 0:2, k], w[:, k, :], start=k == 0, stop=k == KC - 1)
                        close_turn(("ada", s), mm)
                        release(1)
                pe.wait_ge(params_in.sem, params_in.after(l, 16 * PARAM_DMAS))
                a = open_turn(l, "params")
                close_turn("params", pe.transpose(a[:, 0:R_ALL], par_rows[:, :], ident[0:R_ALL, 0:R_ALL]))
                a = open_turn(l, "turned")
                for n in range(6):
                    pe.transpose(a[:, n * P:(n + 1) * P], ws_in[:, n, :], ident)
                for n in range(2):
                    mm = pe.transpose(a[:, (6 + n) * P:(7 + n) * P], past[:, n, :], ident)
                close_turn("turned", mm)
                a = open_turn(l, "filt1")
                carry_waits(pe, "pe")
                mm = product(a[0:HID], [f_w1[:, :]], [cst[0:EMB, C_Z:C_Z + T]])
                close_turn("filt1", mm)
                a = open_turn(l, "mod")
                pe.wait_ge(adac_ready.sem, adac_ready.after(l, N_ADA))
                carry_waits(pe, "pe")
                for n in range(6 * KC):
                    mm = pe.transpose(a[:, 2 * n:2 * n + 2], mod_rows[0:2, n * P:(n + 1) * P], ident[0:2, 0:2])
                close_turn("mod", mm)
                root_mean(l, "norm1", 0)
                a = open_turn(l, "filt2")
                pe.wait_ge(sin_ready.sem, sin_ready.after(l, 1))
                carry_waits(pe, "pe")
                mm = product(a[0:HID], [f_w2[:, :]], [hid[0:HID, 0, :]])
                close_turn("filt2", mm)

                wq, wkv, wv, wu = (chunk_arrived(l, CH_Q + s) for s in range(4))
                wkv = ring[:, 1, 0:KC * KV_COLS].rearrange("p (k n) -> p k n", k=KC)
                for j in range(TILES):
                    a = open_turn(l, ("token", j))
                    for at, w, n in ((0, wq, Q_RANK), (Q_RANK, wkv, KV_COLS), (512, wv, A_W)):
                        for k in range(KC):
                            if (j, at) == (0, 0):
                                pe.wait_ge(h_ready.sem, h_ready.after(l, k + 1))
                            mm = pe.matmul(a[:, at:at + n], h_t[:, k, j * P:(j + 1) * P], w[:, k, 0:n],
                                           start=k == 0, stop=k == KC - 1)
                    close_turn(("token", j), mm)
                release(3)
                for c in range(2):
                    a = open_turn(l, ("u", c))
                    mm = product(a, blocks(wu, c * P), h_k)
                    close_turn(("u", c), mm)
                release(1)
                for c in range(6):
                    a = open_turn(l, ("conv", c))
                    w = chunk_arrived(l, CH_B + c // 2)
                    mm = product(a, blocks(w, c % 2 * P), h_k)
                    close_turn(("conv", c), mm)
                    if c % 2:
                        release(1)
                    if c == 1:
                        for name, tiles in (("filt3a", (0, 1, 2)), ("filt3b", (3, 4))):
                            a = open_turn(l, name)
                            pe.wait_ge(sin_ready.sem, sin_ready.after(l, 2))
                            for n, j in enumerate(tiles):
                                mm = pe.matmul(a[:, n * 512:(n + 1) * 512], hid[0:HID, 1, j * P:(j + 1) * P], f_w3[:, :],
                                               start=True, stop=True)
                            close_turn(name, mm)

                pe.wait_ge(taps_ready.sem, taps_ready.after(l, 1))
                carry_waits(pe, "pe")
                release(1)

                a = open_turn(l, "mix_a")
                pe.wait_ge(zc_ready.sem, zc_ready.after(l, TILES))
                pe.wait_ge(turned_ready.sem, turned_ready.after(l, 1))
                for c in range(2):
                    for j in range(TILES):
                        at = (c * TILES + j) * P
                        for g in (2 * c, 2 * c + 1):
                            out = a[(g % 2) * 64:(g % 2) * 64 + 64, at:at + P]
                            pe.matmul(out, v_tok[:, j, g * 64:(g + 1) * 64], turned[:, g, :], start=True, stop=False)
                            mm = pe.matmul(out, one_row[:, :], abs_row[:, g, :], start=False, stop=True)
                close_turn("mix_a", mm)

                a = open_turn(l, "hy_turn")
                pe.wait_ge(x1v_ready.sem, x1v_ready.after(l, 1))
                for j in range(TILES):
                    for c in range(2):
                        at = (j * 2 + c) * P
                        mm = pe.transpose(a[:, at:at + P], cv[:, 2 + c, j * P:(j + 1) * P], ident)
                close_turn("hy_turn", mm)
                pe.wait_ge(lat_ready.sem, lat_ready.after(l, 1))
                for name, tiles in (("at_turn0", (0, 1, 2)), ("at_turn1", (3, 4))):
                    a = open_turn(l, name)
                    for n, j in enumerate(tiles):
                        for b in range(4):
                            mm = pe.transpose(a[:, n * 512 + b * P:n * 512 + (b + 1) * P],
                                              zc[:, j, b * P:(b + 1) * P], ident)
                    close_turn(name, mm)
                pe.wait_ge(hyu_ready.sem, hyu_ready.after(l, 1))

                def transform(s):
                    return chunk_arrived(l, CH_DFT + s).rearrange("p k n -> p (k n)")\
                        .rearrange("p (j n) -> p j n", j=STILES)

                cos, sin = transform(0), transform(1)
                for q in range(TILES):
                    a = open_turn(l, ("dft", q))
                    for at, lo, big, small in ((0, 0, cos, 0), (512, B_W, sin, 1)):
                        if q < STILES:
                            for j in range(STILES):
                                mm = pe.matmul(a[:, at:at + 512], big[:, j, q * P:(q + 1) * P], hy[:, j, lo:lo + 512],
                                               start=j == 0, stop=j == STILES - 1)
                        else:
                            w = cst[:, C_DFT + small * P:C_DFT + (small + 1) * P]
                            mm = pe.matmul(a[:, at:at + 512], w, hy[:, STILES, lo:lo + 512], start=True, stop=True)
                    close_turn(("dft", q), mm)
                    if q == STILES - 1:
                        release(2)
                icos, isin = transform(2), transform(3)
                pe.wait_ge(yf_ready.sem, yf_ready.after(l, 1))
                for c in range(2):
                    a = open_turn(l, ("idft", c))
                    for n, (m, at) in enumerate([(m, at) for m in range(STILES) for at in (0, B_W)]):
                        w = icos if at == 0 else isin
                        pe.matmul(a[:, 0:SAMPLE], y_f[:, m, at + c * P:at + (c + 1) * P], w[:, m, :],
                                  start=n == 0, stop=n == 2 * STILES - 1)
                    for n, at in enumerate((0, B_W)):
                        w = cst[:, C_DFT + (2 + n) * P:C_DFT + (3 + n) * P]
                        mm = pe.matmul(a[:, SAMPLE:T], y_f[:, STILES, at + c * P:at + (c + 1) * P], w,
                                       start=n == 0, stop=n == 1)
                    close_turn(("idft", c), mm)
                release(2)

                pe.wait_ge(lat_t_ready.sem, lat_t_ready.after(l, 1))
                a = open_turn(l, "rope")
                close_turn("rope", pe.matmul(a[:, 0:SAMPLE], cst[:, C_PERM:C_PERM + P], kt[:, 1, 0:SAMPLE],
                                             start=True, stop=True))
                zq_k = [zq_t[:, k, :] for k in range(2)]
                pe.wait_ge(uq_ready.sem, uq_ready.after(l, 1))
                for h in range(HEADS):
                    a = open_turn(l, ("q", h))
                    close_turn(("q", h), product(a, [uq[:, k, h, :] for k in range(2)], zq_k))

                def open_side(name):
                    pe.wait_ge(side_free.sem, side_free.after(l, SIDE[name]))

                def head_keys(h):
                    open_side(("K", h))
                    for lo, hi in ((0, SAMPLE), (SAMPLE, T + PAST)):
                        mm = pe.matmul(side[0:NOPE, lo:hi], uk[:, h * NOPE:(h + 1) * NOPE], kt[:, 0, lo:hi],
                                       start=True, stop=True)
                    mm.then_inc(side_full.sem, 1)

                def scores(m):
                    h, j = m // TILES, m % TILES
                    a = open_turn(l, ("S", m))
                    if j == 0:
                        pe.wait_ge(k_ready.sem, k_ready.after(l, h + 1))
                    keys = ((0, 0, SAMPLE), (SAMPLE, T, T + PAST)) if j < STILES else ((0, SAMPLE, T),)
                    for at, lo, hi in keys:
                        mm = pe.matmul(a[:, at:at + hi - lo], q_t[:, h, j * P:(j + 1) * P], k_h[h % 2][:, lo:hi],
                                       start=True, stop=True)
                    close_turn(("S", m), mm)

                def turn_probs(m):
                    open_side(("T", m))
                    pe.wait_ge(prob_ready.sem, prob_ready.after(l, m + 1))
                    for b in range(TILES if m % TILES < STILES else 1):
                        mm = pe.transpose(side[:, b * P:(b + 1) * P], prob[:, m % 3, b * P:(b + 1) * P], ident)
                    mm.then_inc(side_full.sem, 1)

                def values(m):
                    h, b = m // TILES, m % TILES
                    if b == 0:
                        pe.wait_ge(side_free.sem, side_free.after(l, SIDE[("T", h * TILES + TILES - 1)] + 1))
                        if h:
                            pe.wait_ge(ol_ready.sem, ol_ready.after(l, h))
                    w = zc[:, b, Q_RANK:Q_RANK + KV_RANK] if b < STILES else past[:, 0, :]
                    pe.matmul(values_at[0][2], w, prob_t[h % 2][:, b, :], start=b == 0, stop=b == TILES - 1)
                    if b == TILES - 1:
                        pe.matmul(values_at[1][2], zc[:, STILES, Q_RANK:Q_RANK + KV_RANK], prob_tp[h % 2],
                                  start=True, stop=True).then_inc(values_full.sem, 1)

                def head_out(i):
                    open_side(("Y", i))
                    for h in (2 * i, 2 * i + 1):
                        pe.wait_ge(ol_ready.sem, ol_ready.after(l, h + 1))
                        lo = h % 2 * VD
                        mm = product(side[lo:lo + VD], [uv[:, h * VD:(h + 1) * VD]], [ol_t[:, h % 2, :]])
                    mm.then_inc(side_full.sem, 1)

                pe.wait_ge(rope_ready.sem, rope_ready.after(l, 1))
                head_keys(0)
                pe.wait_ge(q_ready.sem, q_ready.after(l, HEADS))
                pe.wait_ge(yb_ready.sem, yb_ready.after(l, 1))
                for m in range(STEPS):
                    if m < PAIRS:
                        scores(m)
                    if 2 <= m < PAIRS + 2:
                        turn_probs(m - 2)
                    if VALUES_LAG <= m < PAIRS + VALUES_LAG:
                        values(m - VALUES_LAG)
                    for kind, n in side_turns(m):
                        if kind == "K":
                            head_keys(n)
                        elif kind == "Y":
                            head_out(n)
                pe.wait_ge(yc_ready.sem, yc_ready.after(l, HEADS // 2))
                pe.wait_ge(ya_ready.sem, ya_ready.after(l, 1))
                pe.wait_ge(yb_ready.sem, yb_ready.after(l, 1))

                y_k = [[u_t[:, k, :] for k in range(2)], [cv[:, 2 + k, :] for k in range(2)],
                       yc_k]
                carry_waits(pe, "pe")
                with pe.Fori(0, D // CW) as i:
                    for b in range(3):
                        wg = chunk_arrived(l, CH_GATE + b, i)
                        wb = ring[:, 3, :].rearrange("p (k n) -> p k n", k=KC)
                        for half in range(2):
                            name = ("gate", 2 * b + half)
                            a = open_turn(l, name, i * 3)
                            cols = slice(half * P, (half + 1) * P)
                            halves = ((0, SAMPLE, 0, 512), (SAMPLE, T, 1024, 1024 + P))
                            for lo, hi, at_g, _ in halves:
                                for k in range(KC):
                                    pe.matmul(a[:, at_g:at_g + hi - lo], wg[:, k, cols], h_t[:, k, lo:hi],
                                              start=k == 0, stop=k == KC - 1)
                            if name == ("gate", 0):
                                pe.wait_ge(branch_in.sem, branch_in.after(l, 48) + i * 48)
                            n = len(y_k[b])
                            for lo, hi, _, at_y in halves:
                                for k in range(n):
                                    mm = pe.matmul(a[:, at_y:at_y + hi - lo], wb[:, (0, 2, 4)[b] + k, cols],
                                                   y_k[b][k][:, lo:hi], start=k == 0, stop=k == n - 1)
                            close_turn(name, mm)
                        release(2 if b == 2 else 1)
                pe.wait_ge(merged_ready.sem, merged_ready.after(l, 3 * KC))
                for n in range(KC):
                    a = open_turn(l, ("out", n))
                    w = chunk_arrived(l, CH_OUT + n // 2)
                    mm = product(a, blocks(w, n % 2 * P), [m_t[:, k, :] for k in range(KC)])
                    close_turn(("out", n), mm)
                    if n % 2:
                        release(1)

                root_mean(l, "norm2", KC)
                with pe.Fori(0, 2) as i:
                    for s in range(SLOTS):
                        w = chunk_arrived(l, CH_PQ + s, i)
                        for half in range(2):
                            name = ("pq", 2 * s + half)
                            a = open_turn(l, name, i * 4)
                            mm = product(a, blocks(w, half * P), h_k,
                                         h_ready.after(l, KC) if (s, half) == (0, 0) else None)
                            close_turn(name, mm)
                        release(1)
                pe.wait_ge(pq_ready.sem, pq_ready.after(l, 2 * PH))

                def key_scores(name, n, more, queries):
                    a = open_turn(l, name, more)
                    for g in range(PH):
                        mm = pe.matmul(a[:, g * P:(g + 1) * P], queries[:, g, :], turned[:, 4 + g % 2, :],
                                       start=True, stop=True)
                    close_turn(name, mm)

                def tokens(name, more, tile):
                    a = open_turn(l, name, more)
                    for k in range(KC):
                        mm = pe.transpose(a[:, k * P:(k + 1) * P], tile[:, k, :], ident)
                    close_turn(name, mm)

                for n in range(2):
                    key_scores(("key", n), n, 0, pq_t[:, n * PH:(n + 1) * PH, 0:P])
                tokens("tok", 0, h_t[:, :, 0:P])

                def staged(j, n):
                    pe.wait_ge(stage_ready.sem, stage_ready.after(l, n + 1) + j * 3)

                def peer_tile(j, out, more, following):
                    for h in range(PH):
                        if following and h < 2:
                            staged(j, h)
                            key_scores(("next_key", h), h, j * 2, stage)
                        if following and h == H_TOK + 1:
                            staged(j, 2)
                            tokens("next_tok", j * 2, stage)
                        pe.wait_ge(diag_ready.sem, diag_ready.after(l, h + 1) + j * PH)
                        for k in range(TOPK):
                            n = h * TOPK + k
                            s = n % ROWS_V
                            pe.wait_ge(rows_v_in[s].sem,
                                       rows_v_in[s].after(l, 16 * (n // ROWS_V + 1)) + j * (16 * EXPERTS // ROWS_V))
                            for half in range(2):
                                cols = slice(half * 512, (half + 1) * 512)
                                mm = pe.matmul(y_acc[:, cols], diag[h % 2][:, k, :], rows_v[:, s, cols],
                                               start=n == 0, stop=n == EXPERTS - 1)
                            mm.then_inc(rows_v_free.sem, 1)
                    pe.drain().then_inc(y_full.sem, 1)
                    a = open_turn(l, out, more)
                    pe.wait_ge(ytok_ready.sem, ytok_ready.after(l, 1) + j)
                    for k in range(KC):
                        mm = pe.transpose(a[:, k * P:(k + 1) * P], y_tok[:, k * P:(k + 1) * P], ident)
                    close_turn(out, mm)

                with pe.Fori(0, TILES - 1) as j:
                    peer_tile(j, "peer_out", j * 2, True)
                peer_tile(TILES - 1, "peer_last", 0, False)

            last = FIRST_TURNS + LAYERS * TURNS
            pe.wait_ge(acc_free[last % 2], last // 2 + 1)
            for lo, hi in ((0, SAMPLE), (SAMPLE, T)):
                for k in range(KC):
                    pe.wait_ge(sq_ready.sem, sq_ready.after(LAYERS, k + 1))
                    mm = pe.matmul(accs[last % 2][:, lo:hi], mean_w[:], m_t[:, k, lo:hi], start=k == 0, stop=k == KC - 1)
            mm.then_inc(acc_full[last % 2], 1)
            pe.wait_ge(fin_ready, 1)
            for j in range(TILES):
                g = last + 1 + j
                pe.wait_ge(acc_free[g % 2], g // 2 + 1)
                for k in range(KC):
                    mm = pe.transpose(accs[g % 2][:, k * P:(k + 1) * P], h_t[:, k, j * P:(j + 1) * P], ident)
                mm.then_inc(acc_full[g % 2], 1)

        @block.scalar
        def _(act):
            def full(l, name, more=0):
                act.wait_ge(acc_full[TURN[name] % 2], turn_value(l, name, more))
                return acc(name)

            def give_back(name):
                return acc_free[TURN[name] % 2]

            g = TILES
            act.wait_ge(acc_full[g % 2], g // 2 + 1)
            flat = cond_t[:].rearrange("p a k -> p (a k)")
            act.activation(flat[:, 0:2 * KC], accs[g % 2][:, 0:2 * KC], ACT.Silu).then_inc(cond_ready, 1)
            act.copy(flat[:, 2 * KC:], accs[g % 2][:, 2 * KC:3 * KC]).then_inc(cond_ready, 1)
            act.wait_ge(cond_ready, 2)
            act.sem_inc(acc_free[g % 2], 1)
            act.wait_ge(par_zero, 1)
            act.wait_ge(setup_done, 4)
            act.wait_ge(x_ready, TILES)

            def squares(l, first):
                for k in range(KC):
                    act.activation(m_t[:, k, :], x_t[:, k, :], ACT.Square).then_inc(sq_ready.sem, 1)

            def norm_root(l, name, first):
                a = full(l, name)
                act.activation(root[:, :], a[:, 0:T], ACT.Sqrt, bias=eps_t[:, :]).then_inc(root_ready.sem, 1)
                act.wait_ge(root_ready.sem, root_ready.after(l, first + 1))
                act.sem_inc(give_back(name), 1)

            def add_shift(l, first, shift):
                which = first // KC
                for k in range(KC):
                    act.wait_ge(scaled.sem, scaled.after(l, first + k + 1))
                    act.activation(h_t[:, k, 0:SAMPLE], h_t[:, k, 0:SAMPLE], ACT.Identity,
                                   bias=mod[:, shift + k, 0:1], scale=amp[:, which, k, 0:1])
                    act.activation(h_t[:, k, SAMPLE:T], h_t[:, k, SAMPLE:T], ACT.Identity,
                                   bias=mod[:, shift + k, 1:2], scale=amp[:, which, k, 1:2]).then_inc(h_ready.sem, 1)

            with act.Fori(0, LAYERS) as l:
                def put(dst, src):
                    act.dma_start(dst, src).then_inc(params_in.sem, 16)

                def as_rows(v):
                    return v.rearrange("(k p) -> k p", p=P)

                put(par_rows[R_ADA:R_N1, :], as_rows(b_ada[l]))
                put(par_rows[R_N1:R_N2, :], as_rows(norm1[l]))
                put(par_rows[R_N2:R_CW, :], as_rows(norm2[l]))
                put(par_rows[R_CW:R_CB, :], b_conv_w[l].rearrange("w (k p) -> (w k) p", p=P))
                put(par_rows[R_CB:R_SK, :], as_rows(b_conv_b[l]))
                put(par_rows[R_SK:R_QN, :], as_rows(b_skip[l]))
                put(par_rows[R_QN:R_B1, :], as_rows(q_norm[l]))
                put(par_rows[R_B1:R_B2, 0:HID], b_filt_b1[bass.ds(l, 1), :])
                put(par_rows[R_B2:R_ALL, 0:HID], b_filt_b2[bass.ds(l, 1), :])
                put(kvn[:, :], kv_norm[bass.ds(l, 1), :].to_broadcast([P, KV_RANK]))
                put(abs_row[:, :, :], a_bs[bass.ds(l, 1)])
                put(ws_in[:, 0:4, :], a_ws[l].rearrange("g p q -> p g q"))
                put(ws_in[:, 4:6, :], peer_sub_keys[l].rearrange("s n k -> n s k"))
                put(uk[:, :], w_uk[l].rearrange("c h n -> c (h n)"))
                put(past[:, 0, :], cache_ckv[0, l])
                for r in range(4):
                    put(past[:, 1, r * ROPE:(r + 1) * ROPE], cache_kpe[0, l])
                put(uv[:, :], w_uv[l].rearrange("c h n -> c (h n)"))
                for k in range(2):
                    put(uq[:, k, :, 0:QH], w_uq[l, k * P:(k + 1) * P, :].rearrange("p (h n) -> p h n", h=HEADS))
                put(f_w1[:, :], b_filt_w1[l])
                put(f_w2[:, :], b_filt_w2[l])
                put(f_w3[:, :], b_filt_w3[l])

                def sine(n):
                    act.wait_ge(arg_ready.sem, arg_ready.after(l, n + 1))
                    act.activation(hid[0:HID, n, :], hid[0:HID, n, :], ACT.Sin).then_inc(sin_ready.sem, 1)

                squares(l, 0)
                sine(0)
                norm_root(l, "norm1", 0)
                act.wait_ge(mod_ready.sem, mod_ready.after(l, 1))
                add_shift(l, 0, 0)
                sine(1)

                for j in range(TILES):
                    a = full(l, ("token", j))
                    act.activation(v_tok[:, j, :], a[:, 512:512 + A_W], ACT.Gelu_apprx_tanh)
                    act.copy(zc[:, j, 0:Q_RANK + KV_RANK], a[:, 0:Q_RANK + KV_RANK])
                    act.copy(zc[:, j, Q_RANK + KV_RANK:512].rearrange("p (a b) -> p a b", a=4),
                             a[:, None, Q_RANK + KV_RANK:Q_RANK + KV_COLS].to_broadcast([P, 4, ROPE]))
                    act.activation(dump[:, j, 0:Q_RANK], a[:, 0:Q_RANK], ACT.Square, accum_out=ss[:, 0, j:j + 1])
                    act.activation(dump[:, j, Q_RANK:], a[:, Q_RANK:Q_RANK + KV_RANK], ACT.Square,
                                   accum_out=ss[:, 1, j:j + 1]).then_inc(zc_ready.sem, 1)
                    act.wait_ge(zc_ready.sem, zc_ready.after(l, j + 1))
                    act.sem_inc(give_back(("token", j)), 1)
                for n, width in enumerate((Q_RANK, KV_RANK)):
                    last = act.activation(sr[:, n, :], ss[:, n, :], ACT.Sqrt, bias=eps_t[:, :], scale=1.0 / width)
                last.then_inc(ssr_ready.sem, 1)
                for c in range(2):
                    a = full(l, ("u", c))
                    act.activation(u_t[:, c, :], a[:, 0:T], ACT.Gelu_apprx_tanh).then_inc(u_ready.sem, 1)
                    act.wait_ge(u_ready.sem, u_ready.after(l, c + 1))
                    act.sem_inc(give_back(("u", c)), 1)

                a = full(l, "hy_turn")
                act.copy(hy[:, :, B_W:2 * B_W], a[:, 0:TILES * B_W].rearrange("p (j n) -> p j n", j=TILES))\
                    .then_inc(hyu_ready.sem, 1)
                act.wait_ge(hyu_ready.sem, hyu_ready.after(l, 1))
                act.sem_inc(give_back("hy_turn"), 1)
                for q in range(TILES):
                    a = full(l, ("dft", q))
                    act.copy(spec[:, q, :], a[:, 0:1024]).then_inc(spec_ready.sem, 1)
                    act.wait_ge(spec_ready.sem, spec_ready.after(l, q + 1))
                    act.sem_inc(give_back(("dft", q)), 1)

                act.wait_ge(lat_ready.sem, lat_ready.after(l, 1))
                act.dma_start(state_ckv[0, l], zc[:, STILES, Q_RANK:Q_RANK + KV_RANK]).then_inc(state_out.sem, 16)
                act.dma_start(state_kpe[0, l], zc[:, STILES, 384:384 + ROPE]).then_inc(state_out.sem, 16)

                def take_keys(h):
                    act.wait_ge(side_full.sem, side_full.after(l, SIDE[("K", h)] + 1))
                    act.copy(k_h[h % 2][0:NOPE, :], side[0:NOPE, 0:T + PAST]).then_inc(k_ready.sem, 1)
                    act.wait_ge(k_ready.sem, k_ready.after(l, h + 1))
                    act.sem_inc(side_free.sem, 1)

                def exps(m):
                    width = T if m % TILES < STILES else P
                    a = full(l, ("S", m))
                    act.wait_ge(max_ready.sem, max_ready.after(l, m + 1))
                    act.activation(prob[:, m % 3, 0:width], a[:, 0:width], ACT.Exp, bias=stat[:, m % 4, 0:1],
                                   accum_out=stat[:, m % 4, 1:2]).then_inc(exp_ready.sem, 1)
                    act.wait_ge(exp_ready.sem, exp_ready.after(l, m + 1))
                    act.sem_inc(give_back(("S", m)), 1)

                def take_turned(m):
                    h, j = m // TILES, m % TILES
                    act.wait_ge(side_full.sem, side_full.after(l, SIDE[("T", m)] + 1))
                    if j == 0 and h >= 2:
                        act.wait_ge(values_full.sem, values_full.after(l, h - 1))
                    if j < STILES:
                        act.copy(prob_t[h % 2][:, :, j * P:(j + 1) * P],
                                 side[:, 0:T].rearrange("p (b n) -> p b n", b=TILES))
                    else:
                        act.copy(prob_tp[h % 2], side[:, 0:P])
                    act.drain().then_inc(side_free.sem, 1)

                def take_values(h):
                    act.wait_ge(values_full.sem, values_full.after(l, h + 1))
                    if h >= 2:
                        act.wait_ge(side_full.sem, side_full.after(l, SIDE[("Y", h // 2 - 1)] + 1))
                    for lo, hi, at in values_at:
                        ins = act.copy(ol_t[:, h % 2, lo:hi], at)
                    ins.then_inc(ol_ready.sem, 1)

                def take_heads(i):
                    act.wait_ge(side_full.sem, side_full.after(l, SIDE[("Y", i)] + 1))
                    act.copy(yc_k[i], side[:, 0:T]).then_inc(yc_ready.sem, 1)
                    act.wait_ge(yc_ready.sem, yc_ready.after(l, i + 1))
                    act.sem_inc(side_free.sem, 1)

                take_keys(0)
                for m in range(STEPS):
                    if 2 <= m < PAIRS + 2:
                        take_turned(m - 2)
                    if m < PAIRS:
                        exps(m)
                    for kind, n in side_turns(m):
                        if kind == "K":
                            take_keys(n)
                        elif kind == "Y":
                            take_heads(n)
                    v = m - VALUES_LAG
                    if 0 <= v < PAIRS and v % TILES == TILES - 1:
                        take_values(v // TILES)

                with act.Fori(0, D // CW) as i:
                    for n in range(6):
                        a = full(l, ("gate", n), i * 3)
                        act.wait_ge(merged_credit.sem, merged_credit.after(l, n + 1) + i * 6)
                        act.activation(gate_s[:, n % 2, 0:SAMPLE], a[:, 0:SAMPLE], ACT.Sigmoid)
                        act.activation(gate_s[:, n % 2, SAMPLE:T], a[:, 1024:1024 + P], ACT.Sigmoid)\
                            .then_inc(sig_ready.sem, 1)

                act.wait_ge(xmix_ready.sem, xmix_ready.after(l, KC))
                squares(l, KC)
                norm_root(l, "norm2", 1)
                add_shift(l, KC, 3 * KC)
                with act.Fori(0, 2) as i:
                    for n in range(8):
                        a = full(l, ("pq", n), i * 4)
                        act.copy(arena[:, bass.ds(i * (8 * T) + n * T, T)], a[:, 0:T]).then_inc(pq_ready.sem, 1)
                        act.wait_ge(pq_ready.sem, pq_ready.after(l, n + 1) + i * 8)
                        act.sem_inc(give_back(("pq", n)), 1)

                def soft(j):
                    act.wait_ge(soft_in.sem, soft_in.after(l, 1) + j)
                    act.activation(best_e, best_e, ACT.Exp).then_inc(soft_exp.sem, 1)

                def take_tokens(name, more, j):
                    a = full(l, name, more)
                    act.copy(tok_cur, a[:, 0:D]).then_inc(tok_ready.sem, 1)
                    act.wait_ge(tok_ready.sem, tok_ready.after(l, 1) + j)
                    act.sem_inc(give_back(name), 1)

                def put_stage(src):
                    act.copy(stage, src).then_inc(stage_ready.sem, 1)

                def queries(j, n):
                    return pq_t[:, n * PH:(n + 1) * PH, bass.ds(j * P, P)]

                def peer_tile(j, following):
                    for h in range(PH):
                        if following and h == 0:
                            put_stage(queries(j + 1, 0))
                        if following and h == 1:
                            full(l, ("next_key", 0), j * 2)
                            put_stage(queries(j + 1, 1))
                        if following and h == H_TOK:
                            full(l, ("next_key", 1), j * 2)
                            put_stage(h_t[:, :, bass.ds(j * P + P, P)])
                        act.wait_ge(dots_ready.sem, dots_ready.after(l, h + 1) + j * PH)
                        act.activation(acts[:, h * TOPK:(h + 1) * TOPK], dots[:, h * TOPK:(h + 1) * TOPK],
                                       ACT.Gelu_apprx_tanh).then_inc(acts_ready.sem, 1)
                        if following and h == H_TOK:
                            soft(j + 1)
                    if following:
                        take_tokens("next_tok", j * 2, j + 1)
                    act.wait_ge(y_full.sem, y_full.after(l, 1) + j)
                    act.copy(y_tok, y_acc).then_inc(ytok_ready.sem, 1)

                soft(0)
                take_tokens("tok", 0, 0)
                with act.Fori(0, TILES - 1) as j:
                    peer_tile(j, True)
                peer_tile(TILES - 1, False)
                act.wait_ge(state_out.sem, state_out.after(l, 32))
                act.wait_ge(x_done.sem, x_done.after(l, TILES))

            last = FIRST_TURNS + LAYERS * TURNS
            squares(LAYERS, 0)
            act.wait_ge(acc_full[last % 2], last // 2 + 1)
            act.activation(root[:, :], accs[last % 2][:, 0:T], ACT.Sqrt, bias=eps_t[:, :]).then_inc(root_ready.sem, 1)
            act.wait_ge(root_ready.sem, root_ready.after(LAYERS, 1))
            act.sem_inc(acc_free[last % 2], 1)
            for j in range(TILES):
                g = last + 1 + j
                act.wait_ge(acc_full[g % 2], g // 2 + 1)
                act.copy(y_rows[:, j, :], accs[g % 2][:, 0:D]).then_inc(yrow_ready, 1)
                act.wait_ge(yrow_ready, j + 1)
                act.sem_inc(acc_free[g % 2], 1)

        @block.vector
        def _(dve):
            def full(l, name, more=0):
                dve.wait_ge(acc_full[TURN[name] % 2], turn_value(l, name, more))
                return acc(name)

            def give_back(name):
                dve.drain().then_inc(acc_free[TURN[name] % 2], 1)

            groups = ((0, slice(0, SAMPLE)), (1, slice(SAMPLE, T)))

            dve.wait_ge(x_in, 5 * 16)
            for g in range(TILES):
                dve.wait_ge(acc_full[g % 2], g // 2 + 1)
                dve.tensor_copy(x_t[:, :, g * P:(g + 1) * P],
                                accs[g % 2][:, 0:D].rearrange("p (k n) -> p k n", k=KC)).then_inc(x_ready, 1)
                dve.drain().then_inc(acc_free[g % 2], 1)
            dve.wait_ge(setup_done, 4)
            dve.wait_ge(cond_ready, 2)

            def normalise(l, first):
                dve.wait_ge(root_ready.sem, root_ready.after(l, first + 1))
                dve.reciprocal(rinv[:, :], root[:, :])
                dve.drain()
                for k in range(KC):
                    dve.tensor_tensor(h_t[:, k, :], x_t[:, k, :], rinv[:, :], ALU.mult).then_inc(scaled.sem, 1)

            with dve.Fori(0, LAYERS) as l:
                with dve.Fori(0, N_ADA // SLOTS) as i:
                    for n in range(SLOTS):
                        a = full(l, ("ada", n), i * 2)
                        dve.tensor_copy(mod_rows[0:2, bass.ds(i * (SLOTS * CW) + n * CW, CW)], a[0:2, 0:CW])\
                            .then_inc(adac_ready.sem, 1)
                        give_back(("ada", n))
                a = full(l, "params")
                dve.tensor_copy(par[:, :], a[:, 0:R_ALL]).then_inc(par_ready.sem, 1)
                give_back("params")
                a = full(l, "turned")
                dve.tensor_copy(turned[:, :, :].rearrange("p a b -> p (a b)"), a[:, 0:6 * P])
                dve.tensor_copy(kt[:, :, T:T + PAST], a[:, 6 * P:8 * P].rearrange("p (a b) -> p a b", a=2))
                dve.drain().then_inc(turned_ready.sem, 1)
                give_back("turned")
                heads = uq[:].rearrange("p k h n -> p (k h) n")
                to, frm = (heads[:, :, at:at + ROPE].rearrange("p m (a b c) -> p m a b c", a=2, b=2)
                           for at in (QH, NOPE))
                for b in range(2):
                    dve.tensor_copy(to[:, :, :, b, :], frm[:, :, :, 1 - b, :])
                dve.drain().then_inc(uq_ready.sem, 1)

                def sine_argument(n):
                    turns, magic = 0.15915494309189535, 12582912.0
                    two_pi_hi, two_pi_lo, pi = 6.28125, 0.0019353071795864769, 3.1415925
                    name, row = (("filt1", R_B1), ("filt2", R_B2))[n]
                    a = full(l, name)
                    arg, k = hid[0:HID, n, :], cv_flat[0:HID, 0:T]
                    dve.tensor_scalar(arg, a[0:HID, 0:T], par[0:HID, row:row + 1], None, ALU.add)
                    give_back(name)
                    dve.tensor_scalar(k, arg, turns, magic, ALU.mult, ALU.add)
                    dve.drain()
                    dve.tensor_scalar(k, k, magic, None, ALU.subtract)
                    dve.drain()
                    dve.scalar_tensor_tensor(arg, k, -two_pi_hi, arg, ALU.mult, ALU.add)
                    dve.drain()
                    dve.scalar_tensor_tensor(arg, k, -two_pi_lo, arg, ALU.mult, ALU.add)
                    dve.drain()
                    dve.tensor_scalar(arg, arg, pi, -pi, ALU.min, ALU.max).then_inc(arg_ready.sem, 1)

                sine_argument(0)
                a = full(l, "mod")
                dve.tensor_tensor(mod[:, :, :], a[:, 0:96].rearrange("p (n g) -> p n g", g=2),
                                  par[:, R_ADA:R_N1, None].to_broadcast([P, 6 * KC, 2]), ALU.add)
                give_back("mod")
                for n, row in ((0, R_N1), (1, R_N2)):
                    lo = (3 * n + 1) * KC
                    dve.scalar_tensor_tensor(amp[:, n], mod[:, lo:lo + KC, :], 1.0,
                                             par[:, row:row + KC, None].to_broadcast([P, KC, 2]), ALU.add, ALU.mult)
                dve.tensor_copy(g2_all[:, 0:STILES, :],
                                mod[:, None, 5 * KC:6 * KC, 0].to_broadcast([P, STILES, KC]))
                dve.tensor_copy(g2_all[:, STILES, :], mod[:, 5 * KC:6 * KC, 1])
                dve.drain().then_inc(mod_ready.sem, 1)
                normalise(l, 0)
                sine_argument(1)

                dve.wait_ge(ssr_ready.sem, ssr_ready.after(l, 1))
                dve.wait_ge(zc_ready.sem, zc_ready.after(l, TILES))
                dve.reciprocal(sr[:, :, :], sr[:, :, :])
                dve.drain()
                kv = slice(Q_RANK, Q_RANK + KV_RANK)
                for j in range(TILES):
                    dve.tensor_scalar(zc[:, j, 0:Q_RANK], zc[:, j, 0:Q_RANK], sr[:, 0, j:j + 1], None, ALU.mult)
                    dve.scalar_tensor_tensor(zc[:, j, kv], zc[:, j, kv], sr[:, 1, j:j + 1], kvn[:, :],
                                             ALU.mult, ALU.mult)
                dve.drain().then_inc(lat_ready.sem, 1)

                for c in range(6):
                    a = full(l, ("conv", c))
                    w = [par[:, R_CW + tap * 6 + c:R_CW + tap * 6 + c + 1] for tap in range(3)]
                    dve.tensor_scalar(cv[:, c, :], a[:, 0:T], w[1], par[:, R_CB + c:R_CB + c + 1], ALU.mult, ALU.add)
                    dve.drain()
                    for _, cols in groups:
                        lo, hi = cols.start, cols.stop
                        dve.scalar_tensor_tensor(cv[:, c, lo + 1:hi], a[:, lo:hi - 1], w[0], cv[:, c, lo + 1:hi],
                                                 ALU.mult, ALU.add)
                    dve.drain()
                    for _, cols in groups:
                        lo, hi = cols.start, cols.stop
                        dve.scalar_tensor_tensor(cv[:, c, lo:hi - 1], a[:, lo + 1:hi], w[2], cv[:, c, lo:hi - 1],
                                                 ALU.mult, ALU.add)
                    give_back(("conv", c))
                    if c == 1:
                        dve.wait_ge(w_in_slot[CH_WIN % SLOTS].sem,
                                    w_in_slot[CH_WIN % SLOTS].after(l, 16 * (CH_WIN // SLOTS + 1)))
                        window = ring[:, CH_WIN % SLOTS, :].rearrange("p (j n) -> p j n", j=STILES)
                        for name, tiles in (("filt3a", (0, 1, 2)), ("filt3b", (3, 4))):
                            a = full(l, name)
                            for n, j in enumerate(tiles):
                                w = window[:, j, :] if j < STILES else cst[:, C_WIN:C_WIN + 512]
                                dve.tensor_tensor(y_f[:, j, :], a[:, n * 512:(n + 1) * 512], w, ALU.mult)
                            give_back(name)
                        dve.tensor_tensor(hy[:, :, 0:B_W], y_f[:, :, 0:B_W], y_f[:, :, B_W:], ALU.add)
                        dve.tensor_tensor(hy[:, :, 2 * B_W:], y_f[:, :, 0:B_W], y_f[:, :, B_W:], ALU.subtract)
                        dve.drain().then_inc(taps_ready.sem, 1)
                dve.tensor_tensor(cv[:, 2:4, :], cv[:, 2:4, :], cv[:, 4:6, :], ALU.mult).then_inc(x1v_ready.sem, 1)
                a = full(l, "mix_a")
                dve.wait_ge(u_ready.sem, u_ready.after(l, 2))
                for lo, hi in ((0, 512), (512, 1024), (1024, 2 * T)):
                    ins = dve.tensor_tensor(u_flat[:, lo:hi], u_flat[:, lo:hi], a[:, lo:hi], ALU.mult)
                ins.then_inc(ya_ready.sem, 1)
                give_back("mix_a")
                for name, tiles in (("at_turn0", (0, 1, 2)), ("at_turn1", (3, 4))):
                    a = full(l, name)
                    for n, j in enumerate(tiles):
                        for c in range(2):
                            dve.tensor_scalar(zq_t[:, c, j * P:(j + 1) * P], a[:, n * 512 + c * P:n * 512 + (c + 1) * P],
                                              par[:, R_QN + c:R_QN + c + 1], None, ALU.mult)
                        dve.tensor_copy(kt[:, :, j * P:(j + 1) * P],
                                        a[:, n * 512 + 2 * P:n * 512 + 4 * P].rearrange("p (a b) -> p a b", a=2))
                    give_back(name)
                dve.drain().then_inc(lat_t_ready.sem, 1)
                for m in range(TILES):
                    dve.wait_ge(spec_ready.sem, spec_ready.after(l, m + 1))
                    hc, uc, us, hs = (spec[:, m, n * B_W:(n + 1) * B_W] for n in range(4))
                    real, imag = y_f[:, m, 0:B_W], y_f[:, m, B_W:]
                    dve.tensor_tensor(real, uc, hc, ALU.mult)
                    dve.tensor_tensor(tmp_f[:, 0, :], us, hs, ALU.mult)
                    dve.tensor_tensor(imag, uc, hs, ALU.mult)
                    dve.tensor_tensor(tmp_f[:, 1, :], us, hc, ALU.mult)
                    dve.drain()
                    dve.tensor_tensor(real, real, tmp_f[:, 0, :], ALU.subtract)
                    dve.tensor_tensor(imag, imag, tmp_f[:, 1, :], ALU.add)
                    dve.drain()
                dve.drain().then_inc(yf_ready.sem, 1)
                for c in range(2):
                    a = full(l, ("idft", c))
                    dve.scalar_tensor_tensor(cv[:, 2 + c, :], cv[:, 2 + c, :], par[:, R_SK + c:R_SK + c + 1],
                                             a[:, 0:T], ALU.mult, ALU.add)
                    give_back(("idft", c))
                dve.tensor_tensor(cv[:, 2:4, :], cv[:, 2:4, :], cv[:, 0:2, :], ALU.mult).then_inc(yb_ready.sem, 1)

                a = full(l, "rope")
                dve.tensor_tensor(rope_tmp, a[:, 0:SAMPLE], cst[:, C_SIN:C_SIN + SAMPLE], ALU.mult)
                dve.tensor_tensor(kt[:, 1, 0:SAMPLE], kt[:, 1, 0:SAMPLE], cst[:, C_COS:C_COS + SAMPLE], ALU.mult)
                give_back("rope")
                dve.tensor_tensor(kt[:, 1, 0:SAMPLE], kt[:, 1, 0:SAMPLE], rope_tmp, ALU.add)
                dve.drain()
                for n in range(2):
                    dve.tensor_copy(k_h[n][NOPE:P, :], kt[NOPE:P, 1, :])
                dve.drain().then_inc(rope_ready.sem, 1)
                for h in range(HEADS):
                    a = full(l, ("q", h))
                    dve.tensor_tensor(q_t[:, h, :], a[:, 0:T], cst[:, C_Q:C_Q + T], ALU.mult).then_inc(q_ready.sem, 1)
                    give_back(("q", h))

                def take_max(m):
                    a = full(l, ("S", m))
                    dve.tensor_reduce(stat[:, m % 4, 0:1], a[:, 0:T if m % TILES < STILES else P], AX.X, ALU.max,
                                      negate=True).then_inc(max_ready.sem, 1)

                def norm_probs(m):
                    width = T if m % TILES < STILES else P
                    dve.wait_ge(exp_ready.sem, exp_ready.after(l, m + 1))
                    dve.reciprocal(stat[:, m % 4, 2:3], stat[:, m % 4, 1:2])
                    dve.drain()
                    dve.tensor_scalar(prob[:, m % 3, 0:width], prob[:, m % 3, 0:width], stat[:, m % 4, 2:3], None,
                                      ALU.mult).then_inc(prob_ready.sem, 1)

                for m in range(PAIRS + 1):
                    if m:
                        norm_probs(m - 1)
                    if m < PAIRS:
                        take_max(m)

                dve.drain().then_inc(merged_credit.sem, 2)
                with dve.Fori(0, D // CW) as i:
                    for n in range(6):
                        b, half = n // 2, n % 2
                        a = full(l, ("gate", n), i * 3)
                        dve.wait_ge(sig_ready.sem, sig_ready.after(l, n + 1) + i * 6)
                        out = m_flat[:, bass.ds((i * 2 + half) * T, T)]
                        dst = out if b == 0 else gate_y[:, half, :]
                        for lo, hi, at in ((0, SAMPLE, 512), (SAMPLE, T, 1024 + P)):
                            dve.tensor_tensor(dst[:, lo:hi], gate_s[:, half, lo:hi], a[:, at:at + hi - lo], ALU.mult)
                        give_back(("gate", n))
                        if b:
                            dve.tensor_tensor(out, out, gate_y[:, half, :], ALU.add)
                        dve.drain().then_inc(merged_ready.sem, 1)
                        dve.sem_inc(merged_credit.sem, 1)
                for n in range(KC):
                    a = full(l, ("out", n))
                    for g, cols in groups:
                        ins = dve.scalar_tensor_tensor(x_t[:, n, cols], a[:, cols], mod[:, 2 * KC + n, g:g + 1],
                                                       x_t[:, n, cols], ALU.mult, ALU.add)
                    ins.then_inc(xmix_ready.sem, 1)
                    give_back(("out", n))
                normalise(l, 1)

                def best_keys(name, more, n, g0, g1):
                    a = full(l, name, more)
                    carry_waits(dve, "dve")
                    heads = [(g, (n * PH + g) // 2, g % 2) for g in range(g0, g1)]
                    src = [a[:, g * P:(g + 1) * P] for g in range(PH)]
                    rep = [repl[:, g * P:(g + 1) * P] for g in range(PH)]
                    for g, h, side in heads:
                        dve.max(top_v[:, h, side, 0:8], src[g])
                    dve.drain()
                    for g, h, side in heads:
                        dve.match_replace(rep[g], top_v[:, h, side, 0:8], src[g], -3.0e38)
                        dve.max_index(top_i[:, h, side, 0:8], top_v[:, h, side, 0:8], src[g])
                    dve.drain()
                    for g, h, side in heads:
                        dve.max(top_v[:, h, side, 8:16], rep[g])
                    dve.drain()
                    for g, h, side in heads:
                        dve.max_index(top_i[:, h, side, 8:16], top_v[:, h, side, 8:16], rep[g])
                    if g1 == PH:
                        give_back(name)

                def pair_sums():
                    dve.tensor_copy(top_f, top_i)
                    for h in range(PH):
                        dve.tensor_tensor(cand[:, h * 256:(h + 1) * 256].rearrange("p (a b) -> p a b", a=TOPK),
                                          top_v[:, h, 0, :, None].to_broadcast([P, TOPK, TOPK]),
                                          top_v[:, h, 1, None, :].to_broadcast([P, TOPK, TOPK]), ALU.add)
                    dve.drain()

                def max_sums(at):
                    for h in range(PH):
                        dve.max(best_v[:, h, at:at + 8], cand[:, h * 256:(h + 1) * 256])
                    dve.drain()

                def place_sums(at):
                    for h in range(PH):
                        dve.max_index(best_p.rearrange("p (h k) -> p h k", h=PH)[:, h, at:at + 8],
                                      best_v[:, h, at:at + 8], cand[:, h * 256:(h + 1) * 256])
                    dve.drain()

                def drop_best():
                    for h in range(PH):
                        both = cand[:, h * 256:(h + 1) * 256]
                        dve.match_replace(both, best_v[:, h, 0:8], both, -3.0e38)
                    dve.drain()

                def positions():
                    dve.tensor_tensor(best_e, best_v, best_v[:, :, 0:1].to_broadcast([P, PH, TOPK]), ALU.subtract)\
                        .then_inc(soft_in.sem, 1)
                    dve.tensor_scalar(best_a[:, 0, :], best_p, 4, None, ALU.logical_shift_right)
                    dve.tensor_scalar(best_a[:, 1, :], best_p, 15, None, ALU.bitwise_and)
                    dve.drain()
                    dve.tensor_copy(best_f, best_a)
                    dve.drain()

                def match_places(side):
                    dve.tensor_tensor(cand.rearrange("p (n k) -> p n k", k=TOPK),
                                      best_f[:, side, :, None].to_broadcast([P, EXPERTS, TOPK]),
                                      cst[:, None, C_IOTA:C_IOTA + TOPK].to_broadcast([P, EXPERTS, TOPK]),
                                      ALU.is_equal)
                    dve.drain()

                def pick_keys(side):
                    hit = cand.rearrange("p (h n k) -> p h n k", h=PH, k=TOPK)
                    dve.tensor_tensor(hit, hit, top_f[:, :, side, None, :].to_broadcast([P, PH, TOPK, TOPK]),
                                      ALU.mult)
                    dve.drain()

                def sum_keys(side):
                    dve.tensor_reduce(best_i[:, side, :], cand.rearrange("p (n k) -> p n k", k=TOPK), AX.X, ALU.add)
                    dve.drain()

                def indices(j):
                    dve.scalar_tensor_tensor(best_i[:, 0, :], best_i[:, 0, :], float(NKEYS), best_i[:, 1, :],
                                             ALU.mult, ALU.add)
                    dve.drain()
                    dve.tensor_scalar(idx_next, best_i[:, 0, :], table_base[:, :], None, ALU.add)
                    dve.drain()

                def pass_indices():
                    dve.tensor_copy(idx_u, idx_next).then_inc(idx_ready.sem, 1)

                def pass_last():
                    dve.tensor_copy(idx_last, idx_u[:, LAST:]).then_inc(last_ready.sem, 1)

                def gates(j):
                    dve.wait_ge(soft_exp.sem, soft_exp.after(l, 1) + j)
                    dve.tensor_reduce(best_s, best_e, AX.X, ALU.add)
                    dve.drain()
                    dve.reciprocal(best_r, best_s)
                    dve.drain()
                    dve.tensor_tensor(g_next.rearrange("p (h k) -> p h k", h=PH),
                                      best_e, best_r[:, :, None].to_broadcast([P, PH, TOPK]), ALU.mult)

                def select_part(j, h, quarter):
                    at = (h, quarter)
                    if h in (1, 2):
                        best_keys(("next_key", h - 1), j * 2, h - 1, 2 * quarter, 2 * quarter + 2)
                    elif at == (3, 0):
                        pair_sums()
                    elif at == (3, 1):
                        max_sums(0)
                    elif at == (3, 2):
                        place_sums(0)
                    elif at == (3, 3):
                        drop_best()
                    elif at == (4, 0):
                        max_sums(8)
                    elif at == (4, 1):
                        place_sums(8)
                        positions()
                    elif at == (5, 0) or at == (5, 3):
                        match_places(quarter // 3)
                    elif at == (5, 1) or at == (6, 0):
                        pick_keys(h - 5)
                    elif at == (5, 2) or at == (6, 1):
                        sum_keys(h - 5)
                    elif at == (6, 2):
                        indices(j + 1)
                    elif at == (6, 3):
                        gates(j + 1)

                def add_output(j, out, more):
                    a = full(l, out, more)
                    for k in range(KC):
                        at = x_t[:, k, bass.ds(j * P, P)]
                        dve.scalar_tensor_tensor(at, a[:, k * P:(k + 1) * P], g2_cur[:, k:k + 1], at,
                                                 ALU.mult, ALU.add)
                    give_back(out)
                    dve.drain().then_inc(x_done.sem, 1)

                def diagonals(j, h):
                    if h >= 2:
                        dve.wait_ge(rows_v_free.sem, rows_v_free.after(l, (h - 1) * TOPK) + j * EXPERTS)
                    dve.wait_ge(acts_ready.sem, acts_ready.after(l, h + 1) + j * PH)
                    for k in range(TOPK):
                        n = h * TOPK + k
                        ins = dve.tensor_scalar(diag[h % 2][:, k, :], ident, acts[:, n:n + 1],
                                                g_cur[:, n:n + 1], ALU.mult, ALU.mult)
                    ins.then_inc(diag_ready.sem, 1)

                def dot_products(j, h, k0, k1):
                    for k in range(k0, k1):
                        n = h * TOPK + k
                        s = n % ROWS_U
                        dve.wait_ge(rows_u_in[s].sem,
                                    rows_u_in[s].after(l, 16 * (n // ROWS_U + 1)) + j * (16 * EXPERTS // ROWS_U))
                        dve.tensor_tensor_reduce(rows_u[:, s, :], rows_u[:, s, :], tok_cur, 1.0, 0.0, ALU.mult,
                                                 ALU.add, dots[:, n:n + 1]).then_inc(rows_u_free.sem, 1)

                def peer_tile(j, previous, following):
                    dve.drain()
                    dve.tensor_copy(g_cur[:, :], g_next)
                    dve.wait_ge(tok_ready.sem, tok_ready.after(l, 1) + j)
                    for h in range(PH):
                        if h:
                            diagonals(j, h - 1)
                        for quarter in range(4):
                            if following:
                                select_part(j, h, quarter)
                            dot_products(j, h, quarter * TOPK // 4, (quarter + 1) * TOPK // 4)
                        dve.drain().then_inc(dots_ready.sem, 1)
                        if previous is not None and h == 0:
                            add_output(previous, "peer_out", previous * 2)
                        if h == 0:
                            dve.tensor_copy(g2_cur[:, :], g2_all[:].rearrange("p j k -> p (j k)")[:, bass.ds(j * KC, KC)])
                            dve.drain()
                        if h == 3:
                            pass_last()
                    if following:
                        for s in range(ROWS_V):
                            dve.wait_ge(rows_v_in[s].sem, rows_v_in[s].after(l, 16 * LAST // ROWS_V)
                                        + j * (16 * EXPERTS // ROWS_V))
                        carry_waits(dve, "dve")
                        pass_indices()
                    diagonals(j, PH - 1)

                for n in range(2):
                    best_keys(("key", n), 0, n, 0, PH)
                pair_sums()
                max_sums(0)
                place_sums(0)
                drop_best()
                max_sums(8)
                place_sums(8)
                positions()
                for which in range(2):
                    match_places(which)
                    pick_keys(which)
                    sum_keys(which)
                indices(0)
                pass_indices()
                gates(0)
                dve.drain()
                with dve.Fori(0, 1) as j:
                    peer_tile(j, None, True)
                with dve.Fori(0, TILES - 2) as j:
                    peer_tile(j + 1, j, True)
                with dve.Fori(TILES - 2, TILES - 1) as j:
                    peer_tile(j + 1, j, False)
                add_output(TILES - 1, "peer_last", 0)
                dve.tensor_scalar(table_base[:, :], table_base[:, :], float(NKEYS * NKEYS), None, ALU.add)

            dve.wait_ge(root_ready.sem, root_ready.after(LAYERS, 1))
            dve.reciprocal(rinv[:, :], root[:, :])
            dve.drain()
            for k in range(KC):
                dve.scalar_tensor_tensor(h_t[:, k, :], x_t[:, k, :], cond_t[:, 2, k:k + 1], rinv[:, :],
                                         ALU.mult, ALU.mult)
            dve.drain().then_inc(fin_ready, 1)

        @block.gpsimd
        def _(pool):
            pool.memset(par_rows[:, :], 0.0).then_inc(par_zero, 1)
            pool.memset(mean_w[:, :], 1.0 / D).then_inc(setup_done, 1)
            pool.memset(one_row[:, :], 1.0).then_inc(setup_done, 1)
            pool.memset(eps_t[:, :], EPS).then_inc(setup_done, 1)
            pool.memset(table_base[:, :], 0.0).then_inc(setup_done, 1)
            pool.sem_inc(rows_u_free.sem, ROWS_U)
            pool.sem_inc(rows_v_free.sem, ROWS_V)

            def gather(rows, idx, free, came, table, l, j, n, slots):
                s = n % slots
                pool.wait_ge(free.sem, free.after(l, n + 1 - slots) + j * EXPERTS)
                carry_waits(pool, "pool")
                pool.indirect_dma_start(rows[:, s, :], None, table, bass.IndirectOffsetOnAxis(
                    ap=idx, axis=0)).then_inc(came[s].sem, 16)

            u_rows, v_rows = (w.rearrange("l n d -> (l n) d") for w in (peer_u, peer_v))
            with pool.Fori(0, LAYERS) as l:

                def u_row(j, n):
                    gather(rows_u, idx_u[:, n:n + 1], rows_u_free, rows_u_in, u_rows, l, j, n, ROWS_U)

                def v_row(j, n):
                    idx, at = (idx_u, n) if n < LAST else (idx_last, n - LAST)
                    gather(rows_v, idx[:, at:at + 1], rows_v_free, rows_v_in, v_rows, l, j, n, ROWS_V)

                def later_heads(j):
                    for n in range(TOPK, EXPERTS):
                        u_row(j, n)
                        v_row(j, n - TOPK)
                    pool.wait_ge(last_ready.sem, last_ready.after(l, 1) + j)
                    for n in range(LAST, LAST + ROWS_V):
                        v_row(j, n)

                with pool.Fori(0, 1) as j:
                    pool.wait_ge(idx_ready.sem, idx_ready.after(l, 1) + j)
                    for n in range(TOPK):
                        u_row(j, n)
                    later_heads(j)
                with pool.Fori(0, TILES - 1) as j:
                    pool.wait_ge(idx_ready.sem, idx_ready.after(l, 2) + j)
                    for n in range(TOPK):
                        u_row(j + 1, n)
                        if n < TOPK - ROWS_V:
                            v_row(j, LAST + ROWS_V + n)
                    later_heads(j + 1)
                with pool.Fori(TILES - 1, TILES) as j:
                    for n in range(LAST + ROWS_V, EXPERTS):
                        v_row(j, n)


_INS = ['x_prompt', 'x_sample', 'cache_ckv', 'cache_kpe', 'c', 'c_ctx', 'w_ada', 'b_ada', 'norm1', 'norm2', 'w_in',
        'a_ws', 'a_bs', 'b_conv_w', 'b_conv_b', 'b_filt_w1', 'b_filt_b1', 'b_filt_w2', 'b_filt_b2', 'b_filt_w3',
        'b_skip', 'q_norm', 'kv_norm', 'w_uq', 'w_uk', 'w_uv', 'w_branch_a', 'w_branch_b', 'w_branch_c', 'w_out',
        'peer_wq', 'peer_sub_keys', 'peer_u', 'peer_v', 'final_norm']
_OUTS = [((1, PROMPT, D), 'float32'), ((1, SAMPLE, D), 'float32'), ((1, LAYERS, PROMPT, KV_RANK), 'float32'),
         ((1, LAYERS, PROMPT, ROPE), 'float32')]


def shape_constants():
    import math

    import numpy as np

    f32 = np.float32

    def transform(length):
        theta = math.pi * np.outer(np.arange(length), np.arange(length) + 0.5) / length
        return np.cos(theta), np.sin(theta), np.cos(theta).T / length, np.sin(theta).T / length

    def positions(length):
        t = np.linspace(0.0, 1.0, length, dtype=f32)[:, None]
        bands = (EMB - 1) // 2
        f = np.linspace(1e-4, bands - 1, bands, dtype=f32)
        w = (f32(2.0 * math.pi) * np.arange(length, dtype=f32)[:, None] / f32(length)).astype(f32)
        z = np.concatenate([t, np.cos(f * w), -np.sin(f * w)], axis=-1)
        deltas = np.abs(np.linspace(math.log(1e-2) / 0.3, math.log(1e-2) / 1.5, B_W, dtype=f32))
        fwd = np.exp(-t * deltas)
        bwd = fwd.copy()
        bwd[0] = 0.0
        return z.T, np.concatenate([fwd, bwd], axis=1)

    def by_partition(m):
        return m.reshape(STILES, P, -1).transpose(1, 0, 2).reshape(P, -1)

    cst = np.zeros((P, C_ALL), f32)
    cst[:, C_ID:C_ID + P] = np.eye(P)
    cst[:, C_DFT:C_DFT + 4 * P] = np.concatenate(transform(PROMPT), axis=1)
    tok = np.arange(SAMPLE)
    quarter = ROPE // 4
    inv = (f32(10000.0) ** (-np.arange(quarter, dtype=f32) / quarter)).astype(f32)
    for r in range(P):
        axis, half, f = r % ROPE // (2 * quarter), r % (2 * quarter) // quarter, r % quarter
        ang = (tok // 64 if axis == 0 else tok % 64).astype(f32) * inv[f]
        cst[r, C_COS:C_COS + SAMPLE] = np.cos(ang)
        cst[r, C_SIN:C_SIN + SAMPLE] = np.sin(ang)
        other = r + quarter if half == 0 else r - quarter
        cst[other, C_PERM + r] = -1.0 if half == 0 else 1.0
        if r < NOPE:
            cst[r, C_Q:C_Q + T] = SCALE
        elif r < QH:
            cst[r, C_Q:C_Q + SAMPLE] = SCALE * np.cos(ang)
            cst[r, C_Q + SAMPLE:C_Q + T] = SCALE
        else:
            cst[r, C_Q:C_Q + SAMPLE] = SCALE * np.sin(ang) * (-1.0 if half == 0 else 1.0)
    z_s, win_s = positions(SAMPLE)
    z_p, win_p = positions(PROMPT)
    cst[:, C_WIN:C_WIN + 512] = win_p
    cst[0:EMB, C_Z:C_Z + SAMPLE] = z_s
    cst[0:EMB, C_Z + SAMPLE:C_Z + T] = z_p
    cst[:, C_IOTA:C_IOTA + 16] = np.arange(16)
    tables = np.stack([by_partition(m) for m in (win_s, *transform(SAMPLE))]).astype(f32)
    return cst, tables


def kernel(**inputs):
    import numpy as _np
    import concourse.bacc as _bacc
    from concourse import mybir as _mybir
    from concourse.bass_utils import run_bass_kernel_spmd as _run

    nc = _bacc.Bacc("TRN2", target_bir_lowering=False, num_devices=1)
    cst, tables = shape_constants()
    arrays, args = {}, []
    for name, a in [(n, inputs[n]) for n in _INS] + [("consts", cst), ("tables", tables)]:
        a = _np.ascontiguousarray(a)
        arrays[f"in_{name}_dram"] = a
        args.append(nc.dram_tensor(f"in_{name}_dram", a.shape, _mybir.dt.from_np(a.dtype), kind="ExternalInput").ap())
    for i, (shape, dtype) in enumerate(_OUTS):
        dt = _mybir.dt.from_np(_np.dtype(dtype))
        args.append(nc.dram_tensor(f"out_{i}_dram", shape, dt, kind="ExternalOutput").ap())
    build(nc, *args)
    r = _run(nc, [arrays], core_ids=[0])
    return tuple(r.results[0][f"out_{i}_dram"] for i in range(len(_OUTS)))
```
